# Optimizing a Trainium2 kernel written in Bass

```python
import jax, jax.numpy as jnp
from jax import lax
import numpy as np

D_MODEL = 1024
BATCH = 1
SEQ = 2048
DEPTH = 1

CHUNK = 64
Q_BLOCK = 128
D_MIX = D_MODEL
GDN_HEADS = 4
GDN_HEAD_DIM = 128
GDN_WIDTH = GDN_HEADS * GDN_HEAD_DIM
FOX_HEADS = 8
FOX_HEAD_DIM = (D_MIX - GDN_WIDTH) // FOX_HEADS
FOX_WIDTH = FOX_HEADS * FOX_HEAD_DIM
CONV_K = 4
DEEP_ALPHA = (2.0 * DEPTH) ** 0.25
DEEP_BETA = (8.0 * DEPTH) ** -0.25
LN_EPS = 1e-5
NORM_EPS = 1e-6

IN_SIZES = (3 * GDN_WIDTH, GDN_WIDTH, GDN_HEADS, GDN_HEADS,
            FOX_WIDTH, FOX_WIDTH, FOX_WIDTH, FOX_WIDTH, FOX_HEADS)
IN_COLS = sum(IN_SIZES)

kernel_name = "hymba_gdn_fox_deepnorm_layer"

def _split_cols(t, sizes):
    offs = np.cumsum(np.array(sizes))[:-1].tolist()
    return jnp.split(t, offs, axis=-1)

def _causal_short_conv(u, w):
    c = u.shape[-1]
    return lax.conv_general_dilated(
        u, w[:, None, :].astype(u.dtype), window_strides=(1,),
        padding=[(CONV_K - 1, 0)], dimension_numbers=('NWC', 'WIO', 'NWC'),
        feature_group_count=c)

def _gated_deltanet(q, k, v, beta_logit, a_logit, a_log, dt_bias):
    b, s, h, dk = q.shape
    dv = v.shape[-1]
    n = s // CHUNK
    q = q * lax.rsqrt(jnp.sum(q * q, -1, keepdims=True) + NORM_EPS) * (dk ** -0.5)
    k = k * lax.rsqrt(jnp.sum(k * k, -1, keepdims=True) + NORM_EPS)
    beta = jax.nn.sigmoid(beta_logit)
    g = -jnp.exp(a_log) * jax.nn.softplus(a_logit + dt_bias)

    def to_chunks(t):
        t = jnp.moveaxis(t, 2, 1)
        return t.reshape(b, h, n, CHUNK, *t.shape[3:])

    q, k, v, beta, g = to_chunks(q), to_chunks(k), to_chunks(v), to_chunks(beta), to_chunks(g)
    gc = jnp.cumsum(g, axis=-1)
    idx = jnp.arange(CHUNK)
    causal = idx[:, None] >= idx[None, :]
    strict = idx[:, None] > idx[None, :]
    decay = jnp.exp(jnp.where(causal, gc[..., :, None] - gc[..., None, :], -jnp.inf))
    k_beta = k * beta[..., None]
    lmat = jnp.where(strict, jnp.einsum('bhncd,bhnsd->bhncs', k_beta, k) * decay, 0.0)
    rhs = jnp.concatenate([v * beta[..., None], k_beta * jnp.exp(gc)[..., None]], axis=-1)
    sol = lax.linalg.triangular_solve(lmat, rhs, left_side=True, lower=True, unit_diagonal=True)
    value, k_cumdecay = sol[..., :dv], sol[..., dv:]
    attn_intra = jnp.einsum('bhncd,bhnsd->bhncs', q, k) * decay
    q_g = q * jnp.exp(gc)[..., None]
    g_last = gc[..., -1]
    k_end = k * jnp.exp(g_last[..., None] - gc)[..., None]

    xs = tuple(jnp.moveaxis(t, 2, 0) for t in (q_g, value, k_cumdecay, attn_intra, k_end, g_last))

    def step(state, inp):
        qg_c, val_c, kcd_c, intra_c, kend_c, gl_c = inp
        v_new = val_c - jnp.einsum('bhck,bhkv->bhcv', kcd_c, state)
        o_c = (jnp.einsum('bhck,bhkv->bhcv', qg_c, state)
               + jnp.einsum('bhcs,bhsv->bhcv', intra_c, v_new))
        state = state * jnp.exp(gl_c)[..., None, None] + jnp.einsum('bhck,bhcv->bhkv', kend_c, v_new)
        return state, o_c

    state0 = jnp.zeros((b, h, dk, dv), jnp.float32)
    _, o = lax.scan(step, state0, xs)
    o = jnp.moveaxis(o, 0, 2).reshape(b, h, s, dv)
    return jnp.moveaxis(o, 1, 2)

def _forgetting_attention(q, k, v, f_logit, f_bias):
    b, s, h, d = q.shape
    q, k, v = jnp.moveaxis(q, 2, 1), jnp.moveaxis(k, 2, 1), jnp.moveaxis(v, 2, 1)
    log_f = jax.nn.log_sigmoid(f_logit.astype(jnp.float32) + f_bias.astype(jnp.float32))
    cum = jnp.cumsum(jnp.moveaxis(log_f, 2, 1), axis=-1)
    scale = d ** -0.5
    outs = []
    for i in range(s // Q_BLOCK):
        lo, hi = i * Q_BLOCK, (i + 1) * Q_BLOCK
        logits = (jnp.einsum('bhqd,bhkd->bhqk', q[:, :, lo:hi], k[:, :, :hi]).astype(jnp.float32) * scale
                  + cum[:, :, lo:hi, None] - cum[:, :, None, :hi])
        t_pos = lo + jnp.arange(Q_BLOCK)
        s_pos = jnp.arange(hi)
        logits = jnp.where(s_pos[None, :] <= t_pos[:, None], logits, -jnp.inf)
        p = jax.nn.softmax(logits, axis=-1)
        outs.append(jnp.einsum('bhqk,bhkd->bhqd', p.astype(v.dtype), v[:, :, :hi]))
    o = jnp.concatenate(outs, axis=2)
    return jnp.moveaxis(o, 1, 2)

def _hybrid_layer(x, w_in, conv_w, a_log, dt_bias, gdn_norm_w, fox_f_bias, w_out, ln_g, ln_b):
    b, s, _ = x.shape
    f32 = jnp.float32
    proj = jnp.einsum('bsd,dc->bsc', x, w_in)
    qkv_a, z_a, beta_a, dec_a, q_b, k_b, v_b, z_b, f_b = _split_cols(proj, IN_SIZES)

    qkv_a = jax.nn.silu(_causal_short_conv(qkv_a, conv_w))
    q_a, k_a, v_a = jnp.split(qkv_a.astype(f32), 3, axis=-1)
    heads_a = lambda t: t.reshape(b, s, GDN_HEADS, GDN_HEAD_DIM)
    o_a = _gated_deltanet(heads_a(q_a), heads_a(k_a), heads_a(v_a), beta_a.astype(f32),
                          dec_a.astype(f32), a_log.astype(f32), dt_bias.astype(f32))
    o_a = o_a * lax.rsqrt(jnp.mean(o_a * o_a, -1, keepdims=True) + NORM_EPS) * gdn_norm_w.astype(f32)
    y_a = o_a.reshape(b, s, GDN_WIDTH).astype(x.dtype) * jax.nn.silu(z_a)

    heads_b = lambda t: t.reshape(b, s, FOX_HEADS, FOX_HEAD_DIM)
    o_b = _forgetting_attention(heads_b(q_b), heads_b(k_b), heads_b(v_b), f_b, fox_f_bias)
    y_b = o_b.reshape(b, s, FOX_WIDTH) * jax.nn.silu(z_b)

    mix = jnp.concatenate([y_a, y_b], axis=-1)
    sub = jnp.einsum('bsc,cd->bsd', mix, w_out)
    hres = DEEP_ALPHA * x.astype(f32) + sub.astype(f32)
    mu = jnp.mean(hres, -1, keepdims=True)
    var = jnp.mean(jnp.square(hres - mu), -1, keepdims=True)
    out = (hres - mu) * lax.rsqrt(var + LN_EPS) * ln_g.astype(f32) + ln_b.astype(f32)
    return out.astype(x.dtype)

def setup_inputs(seed: int = 0) -> dict:
    key = jax.random.key(seed)
    ks = jax.random.split(key, 11)
    x = jax.random.normal(ks[0], (BATCH, SEQ, D_MODEL), jnp.float32)
    col_scale = np.concatenate([
        np.ones(2 * GDN_WIDTH), np.full(GDN_WIDTH, DEEP_BETA),
        np.ones(GDN_WIDTH + 2 * GDN_HEADS),
        np.ones(2 * FOX_WIDTH), np.full(FOX_WIDTH, DEEP_BETA),
        np.ones(FOX_WIDTH + FOX_HEADS)]).astype(np.float32)
    w_in = (jax.random.normal(ks[1], (DEPTH, D_MODEL, IN_COLS), jnp.float32)
            * (D_MODEL ** -0.5) * jnp.asarray(col_scale))
    conv_w = jax.random.normal(ks[2], (DEPTH, CONV_K, 3 * GDN_WIDTH), jnp.float32) * (CONV_K ** -0.5)
    a_log = jnp.log(jax.random.uniform(ks[3], (DEPTH, GDN_HEADS), jnp.float32, 1.0, 16.0))
    dt = jnp.exp(jax.random.uniform(ks[4], (DEPTH, GDN_HEADS), jnp.float32,
                                    float(np.log(1e-3)), float(np.log(1e-1))))
    dt_bias = dt + jnp.log(-jnp.expm1(-dt))
    gdn_norm_w = 1.0 + 0.1 * jax.random.normal(ks[5], (DEPTH, GDN_HEAD_DIM), jnp.float32)
    fox_f_bias = jax.random.uniform(ks[6], (DEPTH, FOX_HEADS), jnp.float32, 1.0, 4.0)
    w_out = (jax.random.normal(ks[7], (DEPTH, D_MIX, D_MODEL), jnp.float32)
             * (D_MIX ** -0.5) * DEEP_BETA)
    ln_g = 1.0 + 0.1 * jax.random.normal(ks[8], (DEPTH, D_MODEL), jnp.float32)
    ln_b = 0.1 * jax.random.normal(ks[9], (DEPTH, D_MODEL), jnp.float32)
    return {"x": x, "w_in": w_in, "conv_w": conv_w, "a_log": a_log, "dt_bias": dt_bias,
            "gdn_norm_w": gdn_norm_w, "fox_f_bias": fox_f_bias, "w_out": w_out,
            "ln_g": ln_g, "ln_b": ln_b}

def reference(x, w_in, conv_w, a_log, dt_bias, gdn_norm_w, fox_f_bias, w_out, ln_g, ln_b):
    for l in range(DEPTH):
        x = _hybrid_layer(x, w_in[l], conv_w[l], a_log[l], dt_bias[l], gdn_norm_w[l],
                          fox_f_bias[l], w_out[l], ln_g[l], ln_b[l])
    return x


_drawn_inputs = setup_inputs


def setup_inputs(seed=0):
    import zlib

    import numpy as np

    out = dict(_drawn_inputs(seed))
    spreads = {}
    factors = {'fox_f_bias': 127.24}
    for name, (base, spread) in spreads.items():
        noise = np.random.default_rng([zlib.crc32(name.encode()), seed]).standard_normal(out[name].shape)
        drawn = base * np.exp(spread * noise) if base else spread * noise
        out[name] = __import__('jax').numpy.asarray(drawn.astype(out[name].dtype))
    for name, factor in factors.items():
        out[name] = (out[name] * factor).astype(out[name].dtype)
    return out
```

```python
from contextlib import ExitStack

import numpy as np

import concourse.bass as bass
from concourse import mybir

F32 = mybir.dt.float32
F32R = mybir.dt.float32r
BF16 = mybir.dt.bfloat16
ALU = mybir.AluOpType
ACT = mybir.ActivationFunctionType
AX = mybir.AxisListType

P = 128
SEQ = 2048
D_MODEL = 1024
KT = D_MODEL // P
CHUNK = P
NCH = SEQ // CHUNK
NB = SEQ // 512
GH, GD = 4, 128
FH, FD = 8, 64
CONV_K = 4
DEEP_ALPHA = 2.0 ** 0.25
LN_EPS = 1e-5
NORM_EPS = 1e-6
NEG = -1.0e30

BETA, DECAY, FORGET, GATES = 0, 32, 64, 72
CONV_T, ZA_T, ZB_T, VB_T = 0, 12, 16, 20
N_FEAT = 24

CREDIT = 4


def after(n):
    return n + (CREDIT + 1)


def credit(eng, sems):
    for s in sems:
        eng.sem_inc(s, CREDIT)


def flat(ap):
    return ap.rearrange("p a b -> p (a b)")


def wide(cols, n):
    return cols.unsqueeze(2).broadcast_to([cols.shape[0], cols.shape[1], n])


def project(nc, io, scr):
    PAD = 4
    CONV_AT, Z_AT, QK_AT, V_AT, TILES = 1, 13, 21, 29, 33
    with ExitStack() as ctx:
        def sb(name, shape, dt=F32):
            return ctx.enter_context(nc.sbuf_tensor(name, shape, dt))

        def sem(name):
            return ctx.enter_context(nc.semaphore(name))

        x_hi = sb("x_hi", [P, KT, SEQ], F32R)
        x_lo = sb("x_lo", [P, KT, SEQ], F32R)
        w_raw = sb("w_raw", [P, 2, KT * P])
        w_hi = sb("w_hi", [P, 2, KT * P], F32R)
        w_lo = sb("w_lo", [P, 2, KT * P], F32R)
        u = sb("conv_in", [P, PAD + SEQ])
        acc = sb("conv_acc", [P, SEQ])
        res = [sb(f"result{i}", [P, SEQ]) for i in range(2)]
        hi = sb("qk_hi", [P, SEQ], F32R)
        lo = sb("qk_lo", [P, SEQ], F32R)
        taps = sb("taps", [P, 12, CONV_K])
        tap = sb("tap", [P, CONV_K])
        gate_bias = sb("gate_bias", [GATES, 1])
        gate_sign = sb("gate_sign", [GATES, 1])
        gate_mult = sb("gate_mult", [GATES, 1])
        banks = [ctx.enter_context(nc.psum_tensor(f"proj{i}", [P, SEQ], F32)) for i in range(2)]

        x_landed = [sem(f"x_landed{i}") for i in range(2)]
        x_hi_ready = sem("x_hi_ready")
        x_split = sem("x_split")
        taps_landed = sem("taps_landed")
        gate_consts_landed = sem("gate_consts_landed")
        gate_consts_set = sem("gate_consts_set")
        pad_set = sem("pad_set")
        w_landed = [sem(f"w_landed{i}") for i in range(2)]
        pair_free = sem("pair_free")
        w_hi_ready = sem("w_hi_ready")
        w_split = sem("w_split")
        projected = sem("projected")
        bank_read = sem("bank_read")
        u_ready = sem("u_ready")
        conv_step = sem("conv_step")
        conv_ready = sem("conv_ready")
        tanh_ready = sem("tanh_ready")
        result_ready = sem("result_ready")
        hi_ready = sem("hi_ready")
        lo_ready = sem("lo_ready")
        stored = [sem(f"stored{i}") for i in range(2)]
        qk_stored = sem("qk_stored")
        gates_stored = sem("gates_stored")
        gate_mult_ready = sem("gate_mult_ready")
        gate_y_abs = sem("gate_y_abs")
        gate_exp = sem("gate_exp")
        gate_ln = sem("gate_ln")
        gate_log = sem("gate_log")
        gate_log_scaled = sem("gate_log_scaled")
        scan_mask_set = sem("scan_mask_set")
        gate_cum = sem("gate_cum")
        neg_cum_ready = sem("neg_cum_ready")
        beta_ready = sem("beta_ready")

        with nc.Block() as block:
            @block.sync
            def _(sp):
                for par in range(2):
                    sp.sem_inc(stored[par], 16)
                sp.sem_inc(qk_stored, 32)
                for t in range(2):
                    sp.dma_start(w_raw[:, t, :], io["w"][t]).then_inc(w_landed[t], 16)
                for k in range(KT):
                    if k >= 2:
                        sp.wait_ge(x_split, k - 1)
                    sp.dma_start(res[k % 2][:], io["xT"][k]).then_inc(x_landed[k % 2], 16)
                    if k == 1:
                        sp.dma_start(taps[:], io["taps"]).then_inc(taps_landed, 16)
                        sp.wait_ge(gate_consts_set, 1)
                        sp.dma_start(gate_bias[DECAY:DECAY + GH, :], io["dt_bias"]).then_inc(gate_consts_landed, 16)
                        sp.dma_start(gate_bias[FORGET:FORGET + FH, :], io["f_bias"]).then_inc(gate_consts_landed, 16)
                        sp.dma_start(gate_mult[DECAY:DECAY + GH, :], io["a_log"]).then_inc(gate_consts_landed, 16)

                def load_w(t, par):
                    sp.wait_ge(w_split, t - 1)
                    sp.dma_start(w_raw[:, par, :], io["w"][t]).then_inc(w_landed[par], 16)

                load_w(2, 0)
                sp.wait_ge(neg_cum_ready, 1)
                sp.dma_start(scr["neg_cum"], hi[FORGET:FORGET + FH, :].bitcast(F32)).then_inc(gates_stored, 16)
                sp.wait_ge(beta_ready, 1)
                sp.dma_start(scr["gates"], res[0][0:GATES, :]).then_inc(gates_stored, 16)

                def store_results(pairs, first, n_before, place):
                    with sp.Fori(0, pairs) as i:
                        for j in range(2):
                            par = (first + j) % 2
                            load_w(i * 2 + (first + j + 2), par)
                            sp.wait_ge(result_ready, i * 2 + after(n_before + j))
                            sp.dma_start(scr["feat"][i * 2 + (place + j)], res[par][:]).then_inc(stored[par], 16)

                store_results(6, CONV_AT, 0, CONV_T)
                store_results(4, Z_AT, 12, ZA_T)
                with sp.Fori(0, 4) as i:
                    for j, (h, l) in enumerate((("q_hi", "q_lo"), ("k_hi", "k_lo"))):
                        load_w(i * 2 + (QK_AT + j + 2), (QK_AT + j) % 2)
                        sp.wait_ge(hi_ready, i * 2 + after(j))
                        sp.dma_start(scr[h][i], hi[:].bitcast(F32)).then_inc(qk_stored, 16)
                        sp.wait_ge(lo_ready, i * 2 + after(j))
                        sp.dma_start(scr[l][i], lo[:].bitcast(F32)).then_inc(qk_stored, 16)
                for j in range(4):
                    t = V_AT + j
                    if t + 2 < TILES:
                        load_w(t + 2, t % 2)
                    sp.wait_ge(result_ready, after(20 + j))
                    sp.dma_start(scr["feat"][VB_T + j], res[t % 2][:]).then_inc(stored[t % 2], 16)
                sp.wait_ge(gates_stored, 32)
                sp.wait_ge(qk_stored, 32 + 16 * 16)
                for par in range(2):
                    sp.wait_ge(stored[par], 16 + 16 * 12)

            @block.gpsimd
            def _(pool):
                credit(pool, [w_hi_ready])
                pool.memset(gate_bias[:], 0.0)
                pool.memset(gate_sign[:], 1.0)
                pool.memset(u[:, 0:PAD], 0.0).then_inc(pad_set, 1)
                pool.memset(gate_mult[:], 1.0).then_inc(gate_consts_set, 1)
                pool.wait_ge(gate_consts_set, 1)
                pool.memset(gate_sign[DECAY:DECAY + 32, :], -1.0).then_inc(gate_consts_set, 1)
                pool.wait_ge(gate_consts_set, 2)

                def split(t, par, landed):
                    pool.wait_ge(w_landed[par], landed)
                    if not isinstance(t, int) or t >= 2:
                        pool.wait_ge(projected, t - 1)
                    pool.sem_inc(pair_free, 1)
                    pool.tensor_copy(w_hi[:, par, :], w_raw[:, par, :]).then_inc(w_hi_ready, 1)
                    pool.wait_ge(w_hi_ready, t + after(0))
                    pool.tensor_tensor(w_lo[:, par, :], w_raw[:, par, :], w_hi[:, par, :].bitcast(F32),
                                       ALU.subtract).then_inc(w_split, 1)

                split(0, 0, 16)
                split(1, 1, 16)
                split(2, 0, 32)
                with pool.Fori(0, (TILES - 3) // 2) as i:
                    split(i * 2 + 3, 1, i * 16 + 32)
                    split(i * 2 + 4, 0, i * 16 + 48)

            @block.tensor
            def _(pe):
                def tile(t, par):
                    pe.wait_ge(w_split, t + 1)
                    first = isinstance(t, int)
                    if not first:
                        pe.wait_ge(bank_read, t + (CREDIT - 1))
                    for k in range(KT):
                        if first:
                            pe.wait_ge(x_split, k + 1)
                        for n, (w, x) in enumerate(((w_hi, x_hi), (w_hi, x_lo), (w_lo, x_hi))):
                            for b in range(NB):
                                mm = pe.matmul(banks[par][:, b * 512:(b + 1) * 512], w[:, par, k * P:(k + 1) * P],
                                               x[:, k, b * 512:(b + 1) * 512],
                                               start=(k == 0 and n == 0), stop=(k == KT - 1 and n == 2))
                    mm.then_inc(projected, 1)

                tile(0, 0)
                with pe.Fori(0, (TILES - 1) // 2) as i:
                    tile(i * 2 + 1, 1)
                    tile(i * 2 + 2, 0)

            @block.scalar
            def _(act):
                credit(act, [hi_ready, tanh_ready])
                act.wait_ge(gate_consts_landed, 48)
                act.activation(gate_mult[DECAY:DECAY + GH, :], gate_mult[DECAY:DECAY + GH, :], ACT.Exp)\
                   .then_inc(gate_mult_ready, 1)
                act.wait_ge(gate_y_abs, 1)
                act.activation(res[0][0:GATES, :], acc[0:GATES, :], ACT.Exp, scale=-1.0).then_inc(gate_exp, 1)
                act.wait_ge(gate_exp, 1)
                act.activation(res[0][0:GATES, :], res[0][0:GATES, :], ACT.Ln, bias=1.0).then_inc(gate_ln, 1)
                act.wait_ge(gate_cum, 1)
                act.activation(hi[FORGET:FORGET + FH, :], res[0][FORGET:FORGET + FH, :], ACT.Copy, scale=-1.0)\
                   .then_inc(neg_cum_ready, 1)
                act.activation(res[0][BETA:BETA + GH, :], acc[BETA:BETA + GH, :], ACT.Exp).then_inc(beta_ready, 1)

                act.wait_ge(pad_set, 1)
                act.wait_ge(gates_stored, 32)
                with act.Fori(0, 6) as i:
                    for j in range(2):
                        par = (CONV_AT + j) % 2
                        act.wait_ge(projected, i * 2 + (CONV_AT + j + 1))
                        act.wait_ge(conv_ready, i * 2 + after(j - 1))
                        act.activation(u[:, PAD:], banks[par][:], ACT.Copy).then_inc(u_ready, 1)
                        act.wait_ge(conv_ready, i * 2 + after(j))
                        act.wait_ge(stored[par], i * 16 + 16)
                        act.activation(res[par][:], acc[:], ACT.Tanh, scale=0.5).then_inc(tanh_ready, 1)
                with act.Fori(0, 4) as i:
                    for j in range(2):
                        par = (Z_AT + j) % 2
                        act.wait_ge(projected, i * 2 + (Z_AT + j + 1))
                        act.wait_ge(stored[par], i * 16 + (16 + 6 * 16))
                        act.activation(res[par][:], banks[par][:], ACT.Tanh, scale=0.5).then_inc(tanh_ready, 1)
                with act.Fori(0, 4) as i:
                    for j in range(2):
                        par = (QK_AT + j) % 2
                        act.wait_ge(projected, i * 2 + (QK_AT + j + 1))
                        act.wait_ge(lo_ready, i * 2 + after(j - 1))
                        act.wait_ge(qk_stored, i * 64 + (32 * j + 32))
                        act.activation(hi[:], banks[par][:], ACT.Copy, scale=(FD ** -0.5, 1.0)[j]).then_inc(hi_ready, 1)

            @block.vector
            def _(dve):
                credit(dve, [bank_read, conv_ready, result_ready, lo_ready])
                for k in range(KT):
                    dve.wait_ge(x_landed[k % 2], 16 * (k // 2 + 1))
                    dve.tensor_copy(x_hi[:, k, :], res[k % 2][:]).then_inc(x_hi_ready, 1)
                    dve.wait_ge(x_hi_ready, k + 1)
                    dve.tensor_tensor(x_lo[:, k, :], res[k % 2][:], x_hi[:, k, :].bitcast(F32),
                                      ALU.subtract).then_inc(x_split, 1)
                mask, y = res[1][0:GATES, :], u[0:GATES, PAD:]
                dve.wait_ge(x_split, KT)
                dve.memset(mask, 1.0).then_inc(scan_mask_set, 1)
                dve.wait_ge(scan_mask_set, 1)
                dve.memset(res[1][DECAY:DECAY + GH, :].rearrange("p (c t) -> p c t", t=CHUNK)[:, :, 0:1], 0.0)\
                   .then_inc(scan_mask_set, 1)
                dve.wait_ge(projected, 1)
                dve.wait_ge(gate_consts_set, 2)
                dve.wait_ge(gate_consts_landed, 48)
                dve.tensor_scalar(y, banks[0][0:GATES, :], gate_bias[:], gate_sign[:], ALU.add, ALU.mult)\
                   .then_inc(bank_read, 1)
                dve.wait_ge(bank_read, after(0))
                dve.scalar_tensor_tensor(acc[0:GATES, :], y, -1.0, y, ALU.mult, ALU.max).then_inc(gate_y_abs, 1)
                dve.wait_ge(gate_ln, 1)
                dve.scalar_tensor_tensor(acc[0:GATES, :], y, 0.0, res[0][0:GATES, :], ALU.min, ALU.subtract)\
                   .then_inc(gate_log, 1)
                dve.wait_ge(gate_log, 1)
                dve.wait_ge(gate_mult_ready, 1)
                dve.tensor_scalar(y, acc[0:GATES, :], gate_mult[:], None, ALU.mult).then_inc(gate_log_scaled, 1)
                dve.wait_ge(gate_log_scaled, 1)
                dve.wait_ge(scan_mask_set, 2)
                dve.tensor_tensor_scan(res[0][0:GATES, :], mask, y, 0.0, ALU.mult, ALU.add).then_inc(gate_cum, 1)

                dve.wait_ge(taps_landed, 16)
                dve.wait_ge(beta_ready, 1)
                with dve.Fori(0, 6) as i:
                    for j in range(2):
                        par = (CONV_AT + j) % 2
                        n = i * 2 + j
                        dve.wait_ge(conv_ready, i * 2 + after(j - 1))
                        dve.tensor_copy(tap[:], taps[:, n, :]).then_inc(conv_step, 1)
                        dve.wait_ge(u_ready, i * 2 + (j + 1))
                        dve.wait_ge(conv_step, i * 6 + (3 * j + 1))
                        dve.wait_ge(result_ready, i * 2 + after(j - 1))
                        dve.tensor_scalar(acc[:], u[:, PAD:], tap[:, 3:4], None, ALU.mult).then_inc(bank_read, 1)
                        dve.wait_ge(bank_read, i * 2 + after(CONV_AT + j))
                        for m in range(3):
                            dve.scalar_tensor_tensor(acc[:], u[:, PAD - 3 + m:PAD - 3 + m + SEQ], tap[:, m:m + 1],
                                                     acc[:], ALU.mult, ALU.add)\
                               .then_inc(conv_step if m < 2 else conv_ready, 1)
                            if m < 2:
                                dve.wait_ge(conv_step, i * 6 + (3 * j + 2 + m))
                        dve.wait_ge(conv_ready, i * 2 + after(j))
                        dve.wait_ge(tanh_ready, i * 2 + after(j))
                        dve.scalar_tensor_tensor(res[par][:], res[par][:], 1.0, acc[:], ALU.add, ALU.mult)\
                           .then_inc(result_ready, 1)
                with dve.Fori(0, 4) as i:
                    for j in range(2):
                        par = (Z_AT + j) % 2
                        dve.wait_ge(tanh_ready, i * 2 + after(12 + j))
                        dve.scalar_tensor_tensor(res[par][:], res[par][:], 1.0, banks[par][:], ALU.add, ALU.mult)\
                           .then_inc(result_ready, 1)
                        dve.wait_ge(result_ready, i * 2 + after(12 + j))
                        dve.sem_inc(bank_read, 1)
                with dve.Fori(0, 4) as i:
                    for j in range(2):
                        par = (QK_AT + j) % 2
                        dve.wait_ge(hi_ready, i * 2 + after(j))
                        dve.wait_ge(qk_stored, i * 64 + (32 * j + 32))
                        dve.scalar_tensor_tensor(lo[:], banks[par][:], (FD ** -0.5, 1.0)[j], hi[:].bitcast(F32),
                                                 ALU.mult, ALU.subtract).then_inc(lo_ready, 1)
                        dve.wait_ge(lo_ready, i * 2 + after(j))
                        dve.sem_inc(bank_read, 1)
                for j in range(4):
                    par = (V_AT + j) % 2
                    dve.wait_ge(projected, V_AT + j + 1)
                    dve.wait_ge(stored[par], 16 + 16 * (10 + j // 2))
                    dve.tensor_copy(res[par][:], banks[par][:]).then_inc(result_ready, 1)
                    dve.wait_ge(result_ready, after(20 + j))
                    dve.sem_inc(bank_read, 1)


BODIES = FH // 2
HEAD_UNITS = [(g, kb) for g in range(NB) for kb in range(4 * (g + 1))]
UNITS = 2 * len(HEAD_UNITS)
LAG = 2
SLOTS = UNITS + LAG
PLACES = 3
GROUPS = 2 * NB
CHUNKS = NCH // BODIES
LEVELS = 6
SH = GH // 2
(SS, TVK, TKN, GQ, TX, LEVEL) = range(6)
KS, VN, OD, SUMS, NORM, TY, ITEMS = range(LEVEL + 2 * LEVELS, LEVEL + 2 * LEVELS + 7)


def gdn_at(slot, place):
    n, places = CHUNKS * ITEMS * 2, PLACES * SLOTS
    at = PLACES * slot + place
    return [(k // (2 * ITEMS), k // 2 % ITEMS, k % 2) for k in range(at * n // places, (at + 1) * n // places)]


def level_at(n, i, a):
    return n * (2 * (LEVELS + 1)) + (2 * a + i if i < 2 else 2 * i + a)


def maxima_of(hp, g):
    return [("max", hp, g, a, kb4) for a in range(4) for kb4 in range(g + 1)]


def aux_items():
    at = [[[] for _ in range(PLACES)] for _ in range(SLOTS)]
    for b, s in enumerate((0, 2, 9, 13)):
        at[s][0].append(("v", b))
    for hp in range(2):
        for g in range(NB):
            first = hp * len(HEAD_UNITS) + HEAD_UNITS.index((g, 0))
            count = 4 * (g + 1)
            nxt = (hp, g + 1) if g + 1 < NB else (hp + 1, 0)
            begin, end = (0, max(count - 2, 3)) if g + 1 < NB else (count - 5, count - 2)
            items = maxima_of(*nxt)
            places = [(first + i, q) for i in range(begin, end) for q in range(PLACES)]
            for i, item in enumerate(items):
                s, q = places[i * len(places) // len(items)]
                at[s][q].append(item)
            at[first + end][0].append(("row", *nxt))
            last = first + count - 1
            at[last + LAG][2].append(("sum", hp, g))
            at[min(last + LAG + 1, SLOTS - 1)][2].append(("scale", hp, g))
    return at


AUX_AT = aux_items()
FIRST_AUX = maxima_of(0, 0) + [("row", 0, 0)]
AUX = [x for slot in AUX_AT for place in slot for x in place]
AUX_INDEX = {x: n for n, x in enumerate(FIRST_AUX + AUX)}


def unit(s):
    hp, u = divmod(s, len(HEAD_UNITS))
    g, kb = HEAD_UNITS[u]
    d = kb - 4 * g
    off = P * min(max(d, 0), 2)
    return hp, g, kb, off, d >= 0, slice(0 if d == 3 else P, 2 * P)


def halves(ap, b, odd):
    if len(ap.shape) == 3:
        return ap.rearrange("p h (g two b) -> p h g two b", two=2, b=b)[:, :, :, odd, :]
    return ap.rearrange("p (g two b) -> p g two b", two=2, b=b)[:, :, odd, :]


def blocks(ap, b):
    return ap.rearrange("p h (g b) -> p h g b", b=b) if len(ap.shape) == 3 else ap.rearrange("p (g b) -> p g b", b=b)


STEPS = [k for k in range(ITEMS) if k not in (SUMS, NORM)]


def step_at(n, k, a):
    return n * (2 * len(STEPS)) + (2 * STEPS.index(k) + a + 1)


def mix(nc, io, scr):
    with ExitStack() as ctx:
        def sb(name, shape, dt=F32):
            return ctx.enter_context(nc.sbuf_tensor("m_" + name, shape, dt))

        def bank(name):
            return ctx.enter_context(nc.psum_tensor("m_" + name, [P, 512], F32))

        def sem(name):
            return ctx.enter_context(nc.semaphore("m_" + name))

        ident = sb("ident", [P, P])
        ident_b = sb("ident_b", [P, P], BF16)
        masks = sb("masks", [P, LEVELS + 3, P])
        over_q = sb("over_q", [P, 2 * P], BF16)
        over_k = sb("over_k", [P, 2 * P], BF16)
        ones = sb("ones", [P, FD])
        ones_r = sb("ones_r", [P, 1], F32R)
        half = sb("half", [P, SH])
        norm_w = sb("norm_w", [P, 1])
        half_w = sb("half_w", [P, 1])
        cols = sb("cols", [P, NCH, GATES])
        fcol = sb("fcol", [P, FH, NCH])
        gcol = sb("gcol", [P, NCH, 3 * GH])
        K1 = [sb(f"K1_{i}", [P, SEQ], F32R) for i in range(2)]
        K2 = [sb(f"K2_{i}", [FD + 2, SEQ], F32R) for i in range(2)]
        Q1 = [sb(f"Q1_{i}", [P, 512], F32R) for i in range(4)]
        Q2 = [sb(f"Q2_{i}", [FD + 2, 512], F32R) for i in range(4)]
        QM = [sb(f"QM_{i}", [FD + 2, 512], F32R) for i in range(2)]
        zb = [sb(f"zb_{i}", [FD, 512]) for i in range(2)]
        v_feat = sb("v_feat", [P, SEQ])
        v_hi = sb("v_hi", [P, NCH, 2, FD + 1], F32R)
        v_lo = sb("v_lo", [P, NCH, 2, FD], F32R)
        fbias = [sb(f"fbias{i}", [P, NCH]) for i in range(2)]
        p = [sb(f"p{i}", [P, 512]) for i in range(2)]
        p_hi = [sb(f"p_hi{i}", [P, 512], F32R) for i in range(2)]
        p_lo = [sb(f"p_lo{i}", [P, 512], F32R) for i in range(2)]
        maxima = sb("maxima", [P, 4, 4])
        mcol = sb("mcol", [P, 4], F32R)
        max_diag = sb("max_diag", [P, 4, P], F32R)
        den = sb("den", [1, 512])
        rcol = sb("rcol", [P, 4])
        rec_diag = sb("rec_diag", [P, 4, P])
        gated = sb("gated", [FD, 512])
        yb = [sb(f"yb{i}", [FD, 512]) for i in range(2)]
        H4 = [P, GH, P]
        cin = [sb(f"cin{i}", [P, 12, P]) for i in range(2)]
        grow = [sb(f"grow{i}", H4) for i in range(2)]
        brow = [sb(f"brow{i}", H4) for i in range(2)]
        za = [sb(f"za{i}", H4) for i in range(2)]
        ya = [sb(f"ya{i}", H4) for i in range(2)]
        cc = sb("cc", [P, 3 * GH])
        sq = sb("sq", [P, 2 * GH, P])
        qe, kk, rk, so, ro = ([sb(f"{n}{a}", [P, SH]) for a in range(2)] for n in ("qe", "kk", "rk", "so", "ro"))
        (kn, vb, kT, kend, DT, DTb, eg, LT, intra, qg, X, XT, R2, vn, S, on) = (
            sb(n, H4) for n in ("kn", "vb", "kT", "kend", "DT", "DTb", "eg", "LT", "intra", "qg", "X", "XT", "R2",
                                "vn", "S", "on"))
        C = [sb(f"C{i}", H4) for i in range(LEVELS + 1)]
        T1 = [sb(f"T1_{i}", H4) for i in range(LEVELS)]
        aux = [bank(f"aux{i}") for i in range(2)]
        st = [bank(f"st{i}") for i in range(2)]
        pv = [bank(f"pv{i}") for i in range(2)]
        gd = [bank(f"gd{i}") for i in range(2)]
        gd4 = [b[:].rearrange("p (h t) -> p h t", t=P) for b in gd]
        gd8 = [b[:].rearrange("p (h t) -> p h t", t=P // 2) for b in gd]

        (consts_landed, gates_landed, cols_in_psum, cols_ready, gcol_ready, max_rows_set, ones_set, beta_exp_ready,
         consts_split, rows_set, half_w_ready, zeros_set) = (sem(n) for n in (
             "consts_landed", "gates_landed", "cols_in_psum", "cols_ready", "gcol_ready", "max_rows_set", "ones_set",
             "beta_exp_ready", "consts_split", "rows_set", "half_w_ready", "zeros_set"))
        K_landed = [sem(f"K_landed{i}") for i in range(2)]
        Q_landed = [sem(f"Q_landed{i}") for i in range(4)]
        QM_landed = [sem(f"QM_landed{i}") for i in range(2)]
        zb_landed = [sem(f"zb_landed{i}") for i in range(2)]
        yb_stored = [sem(f"yb_stored{i}") for i in range(2)]
        (v_landed, heads_scored, fbias_ready, aux_ready, aux_used, v_hi_ready, mcol_ready, max_diag_ready, row_ready,
         scores_ready, p_ready, p_hi_ready, p_lo_ready, pv_done, den_ready, rcol_ready, rec_diag_ready, gated_ready,
         yb_ready) = (sem(n) for n in (
             "v_landed", "heads_scored", "fbias_ready", "aux_ready", "aux_used", "v_hi_ready", "mcol_ready",
             "max_diag_ready", "row_ready", "scores_ready", "p_ready", "p_hi_ready", "p_lo_ready", "pv_done",
             "den_ready", "rcol_ready", "rec_diag_ready", "gated_ready", "yb_ready"))
        g_landed = [sem(f"g_landed{i}") for i in range(2)]
        ya_stored = [sem(f"ya_stored{i}") for i in range(2)]
        g_step = sem("g_step")
        (cc_ready, dd0_ready, dd_ready, eg_ready, DT_ready, DTb_ready, sq_ready, kk_ready, rk_ready, kn_ready,
         kT_ready, qg_ready, kend_ready, LT_ready, intra_ready, XT0_ready, X0_ready, R2_ready, vn_ready, sqo_ready,
         so_ready, mo_ready, ro_ready, on_ready, S_ready, ya_ready) = (sem(n) for n in (
             "cc_ready", "dd0_ready", "dd_ready", "eg_ready", "DT_ready", "DTb_ready", "sq_ready", "kk_ready",
             "rk_ready", "kn_ready", "kT_ready", "qg_ready", "kend_ready", "LT_ready", "intra_ready", "XT0_ready",
             "X0_ready", "R2_ready", "vn_ready", "sqo_ready", "so_ready", "mo_ready", "ro_ready", "on_ready",
             "S_ready", "ya_ready"))
        C_ready = sem("C_ready")
        XT_ready = sem("XT_ready")
        T1_ready = sem("T1_ready")

        chunked = {
            "conv": scr["feat"][CONV_T:CONV_T + 12].rearrange("t p (c s) -> c p t s", s=P),
            "za": scr["feat"][ZA_T:ZA_T + GH].rearrange("t p (c s) -> c p t s", s=P),
            "ya": scr["mixT"][0:GH].rearrange("t p (c s) -> c p t s", s=P),
            "gates": scr["gates"].rearrange("r (c s) -> c r s", s=P),
        }
        paired = {n: scr[n].rearrange("i (h d) s -> i h d s", h=2) for n in ("q_hi", "q_lo", "k_hi", "k_lo")}
        paired["zb"] = scr["feat"][ZB_T:ZB_T + 4].rearrange("i (h d) s -> i h d s", h=2)
        paired["yb"] = scr["mixT"][GH:2 * GH].rearrange("i (h d) s -> i h d s", h=2)
        cum_rows = scr["neg_cum"].rearrange("(i h) s -> i h s", h=2)

        with nc.Block() as block:
            @block.sync
            def _(sp):
                for i in range(2):
                    sp.sem_inc(yb_stored[i], 16)
                    sp.sem_inc(ya_stored[i], 16)

                def load_keys(i, hp):
                    sp.dma_start(K1[hp][0:FD, :].bitcast(F32), paired["k_hi"][i][hp]).then_inc(K_landed[hp], 16)
                    sp.dma_start(K2[hp][0:FD, :].bitcast(F32), paired["k_hi"][i][hp]).then_inc(K_landed[hp], 16)
                    sp.dma_start(K1[hp][FD:P, :].bitcast(F32), paired["k_lo"][i][hp]).then_inc(K_landed[hp], 16)
                    sp.dma_start(K2[hp][FD + 1:FD + 2, :].bitcast(F32), cum_rows[i][hp:hp + 1]).then_inc(K_landed[hp], 16)

                def load_max_queries(i, G):
                    hp, g = G // NB % 2, G % NB
                    sp.dma_start(QM[G % 2][0:FD, :].bitcast(F32), paired["q_hi"][i][hp][:, g * 512:(g + 1) * 512])\
                      .then_inc(QM_landed[G % 2], 16)

                def load_queries(i, G):
                    hp, g = G // NB % 2, G % NB
                    b = G % 4
                    cut = slice(g * 512, (g + 1) * 512)
                    for dst, src in ((Q1[b][0:FD, :], "q_hi"), (Q1[b][FD:P, :], "q_hi"), (Q2[b][0:FD, :], "q_lo")):
                        sp.dma_start(dst.bitcast(F32), paired[src][i][hp][:, cut]).then_inc(Q_landed[b], 16)

                def load_z(i, G):
                    hp, g = G // NB % 2, G % NB
                    sp.dma_start(zb[G % 2][:], paired["zb"][i][hp][:, g * 512:(g + 1) * 512]).then_inc(zb_landed[G % 2], 16)

                def load_chunk(n, par):
                    for tile, row in ((grow, DECAY), (brow, BETA)):
                        rows = chunked["gates"][n][row:row + GH].unsqueeze(0).broadcast_to(H4)
                        sp.dma_start(tile[par][:], rows).then_inc(g_landed[par], 16)
                    sp.dma_start(cin[par][:], chunked["conv"][n]).then_inc(g_landed[par], 16)
                    sp.dma_start(za[par][:], chunked["za"][n]).then_inc(g_landed[par], 16)

                gates = flat(cin[0][:])
                sp.dma_start(gates[0:GATES, :], scr["gates"][:, 0:12 * P]).then_inc(gates_landed, 16)
                sp.dma_start(flat(cin[1][:])[0:GATES, 0:SEQ - 12 * P], scr["gates"][:, 12 * P:]).then_inc(gates_landed, 16)
                sp.dma_start(ident[:], io["ident"]).then_inc(consts_landed, 16)
                sp.dma_start(masks[:], io["masks"]).then_inc(consts_landed, 16)
                sp.dma_start(norm_w[:], io["norm_w"]).then_inc(consts_landed, 16)
                sp.wait_ge(rows_set, 2)
                load_max_queries(0, 0)
                load_keys(0, 0)
                load_queries(0, 0)
                sp.wait_ge(cols_in_psum, 4)
                load_chunk(0, 0)
                sp.dma_start(v_feat[:], scr["feat"][VB_T]).then_inc(v_landed, 16)
                load_max_queries(0, 1)
                load_queries(0, 1)
                load_z(0, 0)
                load_z(0, 1)

                with sp.Fori(0, BODIES) as it:
                    after_it = (it + 1) % BODIES
                    for s in range(SLOTS + 1):
                        for G in range(2, GROUPS + 2):
                            if s == (G - 2) // NB * len(HEAD_UNITS) + HEAD_UNITS.index(((G - 2) % NB, 0)):
                                i = it if G < GROUPS else after_it
                                sp.wait_ge(mcol_ready, it * GROUPS + after(G - 2))
                                load_max_queries(i, G)
                                sp.wait_ge(yb_ready, it * GROUPS + after(G - 4))
                                load_queries(i, G)
                        if s == 0:
                            sp.wait_ge(heads_scored, it * 2 + after(-1))
                            load_keys(it, 1)
                        if s == UNITS // 2 + 1:
                            sp.wait_ge(heads_scored, it * 2 + after(0))
                            load_keys(after_it, 0)
                            sp.wait_ge(aux_used, it * len(AUX) + after(AUX_INDEX["v", 3]))
                            sp.dma_start(v_feat[:], scr["feat"][VB_T:VB_T + 4][after_it]).then_inc(v_landed, 16)
                        for j in range(CHUNKS + 1):
                            if s == -(-j * SLOTS // CHUNKS):
                                sp.wait_ge(ya_ready, it * (2 * CHUNKS) + after(2 * (j - 1) + 1))
                                if j > 0:
                                    sp.dma_start(chunked["ya"][it * CHUNKS + (j - 1)], ya[(j - 1) % 2][:])\
                                      .then_inc(ya_stored[(j - 1) % 2], 16)
                                if j < CHUNKS:
                                    load_chunk((it * CHUNKS + (j + 1)) % NCH, (j + 1) % 2)
                        for kind, *what in AUX_AT[s][2] if s < SLOTS else ():
                            if kind == "scale":
                                hp, g = what
                                G = hp * NB + g
                                sp.wait_ge(yb_ready, it * GROUPS + after(G))
                                sp.dma_start(paired["yb"][it][hp][:, g * 512:(g + 1) * 512], yb[G % 2][:])\
                                  .then_inc(yb_stored[G % 2], 16)
                                load_z(it if G + 2 < GROUPS else after_it, G + 2)
                for i in range(2):
                    sp.wait_ge(ya_stored[i], 16 + 16 * NCH // 2)
                    sp.wait_ge(yb_stored[i], 16 + 16 * BODIES * GROUPS // 2)
                    sp.wait_ge(K_landed[i], 64 * (BODIES + 1 - i))
                    sp.wait_ge(g_landed[i], 64 * (NCH // 2 + 1 - i))
                    sp.wait_ge(QM_landed[i], 16 * (BODIES * GROUPS // 2 + 1))
                    sp.wait_ge(zb_landed[i], 16 * (BODIES * GROUPS // 2 + 1))
                    sp.wait_ge(Q_landed[i], 48 * (BODIES * GROUPS // 4 + 1))
                sp.wait_ge(v_landed, 16 * (BODIES + 1))

            @block.tensor
            def _(pe):
                credit(pe, [aux_ready, heads_scored, scores_ready, pv_done])
                pe.wait_ge(gates_landed, 32)
                pe.wait_ge(consts_landed, 48)
                for q, b in enumerate((aux[0], aux[1], st[0], st[1])):
                    for i in range(4):
                        c = 4 * q + i
                        src = flat(cin[c // 12][:])[0:GATES, c % 12 * P:(c % 12 + 1) * P]
                        mm = pe.transpose(b[:, i * P:i * P + GATES], src, ident[0:GATES, 0:GATES])
                    mm.then_inc(cols_in_psum, 1)
                pe.wait_ge(cols_ready, 4)
                pe.wait_ge(consts_split, 5)
                pe.wait_ge(rows_set, 2)
                pe.wait_ge(ones_set, 1)
                pe.wait_ge(zeros_set, 1)

                def do_aux(item, it=0):
                    kind, *what = item
                    m = AUX_INDEX[item]
                    b = aux[m % 2]
                    pe.wait_ge(aux_used, it * len(AUX) + after(m - 2))
                    if kind == "v":
                        if what[0] == 0:
                            pe.wait_ge(v_landed, it * 16 + 16)
                        for i in range(4):
                            c = what[0] * 4 + i
                            mm = pe.transpose(b[:, i * P:(i + 1) * P], v_feat[:, c * P:(c + 1) * P], ident[:])
                    elif kind == "max":
                        hp, g, a, kb4 = what
                        G = hp * NB + g
                        if a == 0 and kb4 == 0:
                            pe.wait_ge(QM_landed[G % 2], it * 64 + (16 * (G // 2) + 16))
                            pe.wait_ge(K_landed[hp % 2], it * 64 + (64 * (hp // 2) + 64))
                        diagonal = kb4 == g
                        n = max(a + 1, 2) * P if diagonal else 512
                        mm = pe.matmul(b[:, 0:n], QM[G % 2][:, a * P:(a + 1) * P],
                                       K2[hp % 2][:, kb4 * 512:kb4 * 512 + n], start=True, stop=not diagonal)
                        if diagonal:
                            mm = pe.matmul(b[:, a * P:n], ident_b[:], over_q[:, 0:n - a * P], start=False, stop=True)
                    elif kind == "row":
                        hp, g = what
                        pe.wait_ge(max_diag_ready, it * GROUPS + after(hp * NB + g))
                        mm = pe.matmul(b[0:1, :], ones_r[:], flat(max_diag[:]), start=True, stop=True)
                    elif kind == "sum":
                        hp, g = what
                        pe.wait_ge(den_ready, it * GROUPS + after(hp * NB + g))
                        for a in range(4):
                            mm = pe.matmul(b[:, a:a + 1], den[:, a * P:(a + 1) * P], ones[0:1, 0:1], start=True, stop=True)
                    else:
                        hp, g = what
                        pe.wait_ge(rec_diag_ready, it * GROUPS + after(hp * NB + g))
                        mm = pe.matmul(b[0:FD, :], ones[:], flat(rec_diag[:]), start=True, stop=True)
                    mm.then_inc(aux_ready, 1)

                for item in FIRST_AUX:
                    do_aux(item)
                with pe.Fori(0, BODIES) as it:
                    def scores(s):
                        hp, g, kb, off, diagonal, cut = unit(s)
                        G = hp * NB + g
                        b = st[s % 2]
                        if kb == 0:
                            pe.wait_ge(Q_landed[G % 4], it * 96 + (48 * (G // 4) + 48))
                            pe.wait_ge(row_ready, it * GROUPS + after(G))
                        pe.wait_ge(p_ready, it * UNITS + after(s - 2))
                        keys = slice(kb * P, (kb + 1) * P)
                        pe.matmul(b[:, off:], K1[hp][:, keys], Q1[G % 4][:, off:], start=True, stop=False)
                        mm = pe.matmul(b[:, off:], K2[hp][:, keys], Q2[G % 4][:, off:], start=False, stop=not diagonal)
                        if diagonal:
                            mm = pe.matmul(b[:, off:off + cut.stop - cut.start], ident_b[:], over_k[:, cut],
                                           start=False, stop=True)
                        mm.then_inc(scores_ready, 1)
                        if s % len(HEAD_UNITS) == len(HEAD_UNITS) - 1:
                            pe.wait_ge(scores_ready, it * UNITS + after(s))
                            pe.sem_inc(heads_scored, 1)

                    def values(s):
                        hp, g, kb, off, diagonal, _ = unit(s)
                        G = hp * NB + g
                        b = pv[G % 2]
                        if kb == 0:
                            pe.wait_ge(gated_ready, it * GROUPS + after(G - 2))
                        pe.wait_ge(p_hi_ready, it * UNITS + after(s))
                        last = kb == 4 * g + 3
                        pe.matmul(b[0:FD + 1, off:], v_hi[:, kb, hp, :], p_hi[s % 2][:, off:], start=kb == 0, stop=False)
                        pe.matmul(b[0:FD, off:], v_lo[:, kb, hp, :], p_hi[s % 2][:, off:], start=False, stop=False)
                        pe.wait_ge(p_lo_ready, it * UNITS + after(s))
                        pe.matmul(b[0:FD + 1, off:], v_hi[:, kb, hp, :], p_lo[s % 2][:, off:], start=False, stop=last)\
                          .then_inc(pv_done, 1)

                    def gdn(j, k, a):
                        n = it * CHUNKS + j
                        m = n * 2 + a
                        par = j % 2
                        b, b64 = gd4[a], gd8[a]
                        heads = range(a * SH, (a + 1) * SH)

                        def product(lhsT, rhs):
                            for i, h in enumerate(heads):
                                mm = pe.matmul(b[:, i, :], lhsT[:, h, :], rhs[:, h, :], start=True, stop=True)
                            return mm

                        def turned(tile):
                            for i, h in enumerate(heads):
                                mm = pe.transpose(b[:, i, :], tile[:, h, :], ident[:])
                            return mm

                        if k == SS:
                            pe.wait_ge(sq_ready, m + after(0))
                            pe.wait_ge(ya_ready, m + after(-2))
                            for i, h in enumerate(heads):
                                pe.matmul(gd[a][:, i:i + 1], sq[:, h, :], ones[:, 0:1], start=True, stop=True)
                                mm = pe.matmul(gd[a][:, SH + i:SH + i + 1], sq[:, GH + h, :], ones[:, 0:1], start=True, stop=True)
                        elif k == TVK:
                            pe.wait_ge(g_landed[par], it * 128 + (64 * (j // 2) + 64))
                            pe.wait_ge(kk_ready, m + after(0))
                            for i, h in enumerate(heads):
                                pe.transpose(b[:, i, :], cin[par][:, 2 * GH + h, :], ident[:])
                                mm = pe.transpose(b[:, SH + i, :], cin[par][:, GH + h, :], ident[:])
                        elif k == TKN:
                            pe.wait_ge(kn_ready, m + after(0))
                            mm = turned(kn)
                        elif k == GQ:
                            pe.wait_ge(kT_ready, m + after(0))
                            for i, h in enumerate(heads):
                                pe.matmul(b[:, i, :], kT[:, h, :], kT[:, h, :], start=True, stop=True)
                                mm = pe.matmul(b[:, SH + i, :], kT[:, h, :], cin[par][:, h, :], start=True, stop=True)
                        elif k == TX:
                            pe.wait_ge(intra_ready, m + after(0))
                            pe.wait_ge(XT0_ready, m + after(0))
                            mm = turned(XT)
                        elif k < KS:
                            lv, part = divmod(k - LEVEL, 2)
                            width = 2 << lv
                            if part == 0:
                                pe.wait_ge(C_ready, level_at(n, lv + 1, a) + after(0))
                                if lv == 0:
                                    pe.wait_ge(X0_ready, m + after(0))
                                else:
                                    pe.wait_ge(XT_ready, n * (2 * LEVELS) + (2 * (lv - 1) + a) + after(0))
                                for i, h in enumerate(heads):
                                    mm = pe.matmul(blocks(b64[:, i, :], width), C[lv + 1][:, h, :],
                                                   halves(X[:, h, :], width, 0), start=True, stop=True)
                            else:
                                pe.wait_ge(T1_ready, n * (2 * LEVELS) + (2 * lv + a) + after(0))
                                for i, h in enumerate(heads):
                                    if lv < LEVELS - 1:
                                        pe.matmul(blocks(b64[:, i, :], width), XT[:, h, :],
                                                  halves(T1[lv][:, h, :], width, 0), start=True, stop=True)
                                    mm = pe.matmul(blocks(b64[:, SH + i, :], width), T1[lv][:, h, :],
                                                   halves(XT[:, h, :], width, 1), start=True, stop=True)
                        elif k == KS:
                            pe.wait_ge(S_ready, m + after(-2))
                            pe.wait_ge(XT_ready, n * (2 * LEVELS) + (2 * (LEVELS - 1) + a) + after(0))
                            mm = product(kT, S)
                        elif k == VN:
                            pe.wait_ge(R2_ready, m + after(0))
                            mm = product(XT, R2)
                        elif k == OD:
                            pe.wait_ge(qg_ready, m + after(0))
                            pe.wait_ge(kend_ready, m + after(0))
                            pe.wait_ge(vn_ready, m + after(0))
                            for i, h in enumerate(heads):
                                pe.matmul(b[:, i, :], qg[:, h, :], S[:, h, :], start=True, stop=False)
                                pe.matmul(b[:, i, :], intra[:, h, :], vn[:, h, :], start=False, stop=True)
                            for i, h in enumerate(heads):
                                mm = pe.matmul(b[:, SH + i, :], kend[:, h, :], vn[:, h, :], start=True, stop=True)
                        elif k == TY:
                            pe.wait_ge(S_ready, m + after(0))
                            pe.wait_ge(on_ready, m + after(0))
                            mm = turned(on)
                        if k not in (SUMS, NORM):
                            mm.then_inc(g_step, 1)

                    def place(s, q):
                        for item in AUX_AT[s][q]:
                            do_aux(item, it)
                        for j, k, a in gdn_at(s, q):
                            gdn(j, k, a)

                    for s in range(SLOTS):
                        if s < UNITS:
                            scores(s)
                        place(s, 0)
                        if s >= LAG:
                            values(s - LAG)
                        place(s, 1)
                        place(s, 2)

            @block.scalar
            def _(act):
                credit(act, [p_ready, eg_ready, DT_ready, sq_ready, kT_ready, X0_ready, T1_ready, vn_ready, sqo_ready])
                act.wait_ge(cols_ready, 4)
                act.activation(gcol[:, :, GH:2 * GH], cols[:, :, DECAY:DECAY + GH], ACT.Exp).then_inc(beta_exp_ready, 1)
                act.wait_ge(gcol_ready, 2)
                act.wait_ge(zeros_set, 1)
                with act.Fori(0, BODIES) as it:
                    def exp(s):
                        hp, g, kb, off, _, _ = unit(s)
                        if s % len(HEAD_UNITS) == 0:
                            act.wait_ge(fbias_ready, it * 2 + (hp + 1))
                        act.wait_ge(p_lo_ready, it * UNITS + after(s - 2))
                        act.wait_ge(scores_ready, it * UNITS + after(s))
                        act.activation(p[s % 2][:, off:], st[s % 2][:, off:], ACT.Exp, bias=fbias[hp][:, kb:kb + 1])\
                           .then_inc(p_ready, 1)

                    def gdn(j, k, a):
                        n = it * CHUNKS + j
                        m = n * 2 + a
                        par = j % 2
                        mine = slice(a * SH, (a + 1) * SH)

                        def take(out, src, ready, func=ACT.Copy):
                            act.wait_ge(g_step, step_at(n, k, a))
                            act.activation(out, src, func).then_inc(ready, 1)

                        if k == SS:
                            act.wait_ge(g_landed[par], it * 128 + (64 * (j // 2) + 64))
                            act.wait_ge(on_ready, m + after(-2))
                            act.activation(sq[:].rearrange("p (w h) t -> p w h t", w=2)[:, :, mine, :],
                                           cin[par][:, 0:2 * GH, :].rearrange("p (w h) t -> p w h t", w=2)[:, :, mine, :],
                                           ACT.Square).then_inc(sq_ready, 1)
                        elif k == TVK:
                            act.wait_ge(S_ready, m + after(-2))
                            act.activation(eg[:, mine, :], grow[par][:, mine, :], ACT.Exp).then_inc(eg_ready, 1)
                            act.wait_ge(dd_ready, m + after(0))
                            act.activation(DT[:, mine, :], DT[:, mine, :], ACT.Exp).then_inc(DT_ready, 1)
                        elif k == TKN:
                            take(kT[:, mine, :], gd4[a][:, 0:SH, :], kT_ready)
                        elif k == TX:
                            take(X[:, mine, :], gd4[a][:, 0:SH, :], X0_ready)
                        elif LEVEL <= k < KS and (k - LEVEL) % 2 == 0:
                            lv = (k - LEVEL) // 2
                            take(halves(T1[lv][:, mine, :], 2 << lv, 0), blocks(gd8[a][:, 0:SH, :], 2 << lv), T1_ready)
                        elif k == VN:
                            take(vn[:, mine, :], gd4[a][:, 0:SH, :], vn_ready)
                        elif k == OD:
                            act.wait_ge(S_ready, m + after(0))
                            take(sq[:, mine, :], gd4[a][:, 0:SH, :], sqo_ready, ACT.Square)

                    for s in range(SLOTS):
                        if s < UNITS:
                            exp(s)
                        for q in range(PLACES):
                            for j, k, a in gdn_at(s, q):
                                gdn(j, k, a)

            @block.gpsimd
            def _(pool):
                credit(pool, [p_lo_ready, dd0_ready, dd_ready, DTb_ready, rk_ready, qg_ready, kend_ready, ro_ready,
                              C_ready, XT0_ready, max_diag_ready, rec_diag_ready])
                for i in range(2):
                    pool.memset(QM[i][FD:FD + 2, :].bitcast(F32), 1.0)
                    pool.memset(K2[i][FD:FD + 2, :].bitcast(F32), 1.0)
                for i in range(4):
                    q2_rows = pool.memset(Q2[i][FD:FD + 2, :].bitcast(F32), 0.0)
                q2_rows.then_inc(max_rows_set, 1)
                pool.wait_ge(max_rows_set, 1)
                for i in range(2):
                    pool.memset(QM[i][FD:FD + 1, :].bitcast(F32), 0.0).then_inc(rows_set, 1)
                pool.wait_ge(rows_set, 2)
                pool.memset(v_hi[:, :, :, FD:].bitcast(F32), 1.0)
                pool.memset(ones[:], 1.0)
                pool.memset(ones_r[:].bitcast(F32), 1.0)
                pool.memset(half[:], -0.5)
                pool.memset(S[:], 0.0).then_inc(ones_set, 1)
                pool.wait_ge(ones_set, 1)
                for i in range(LEVELS + 1):
                    zeroed = pool.memset(C[i][:], 0.0)
                for i in range(LEVELS):
                    zeroed = pool.memset(T1[i][:], 0.0)
                zeroed.then_inc(zeros_set, 1)
                pool.wait_ge(zeros_set, 1)
                pool.wait_ge(consts_landed, 48)
                ident4 = ident[:].unsqueeze(1).broadcast_to([P, 4, P])

                def do_aux(item, it=0):
                    kind, *what = item
                    m = AUX_INDEX[item]
                    if kind == "max" and what[2] == 3 and what[3] == what[1]:
                        G = what[0] * NB + what[1]
                        pool.wait_ge(row_ready, it * GROUPS + after(G - 1))
                        pool.wait_ge(mcol_ready, it * GROUPS + after(G))
                        pool.tensor_tensor(max_diag[:], ident4, wide(mcol[:].bitcast(F32), P), ALU.mult)\
                            .then_inc(max_diag_ready, 1)
                    elif kind == "sum":
                        G = what[0] * NB + what[1]
                        pool.wait_ge(yb_ready, it * GROUPS + after(G - 1))
                        pool.wait_ge(rcol_ready, it * GROUPS + after(G))
                        pool.tensor_tensor(rec_diag[:], ident4, wide(rcol[:], P), ALU.mult).then_inc(rec_diag_ready, 1)

                for item in FIRST_AUX:
                    do_aux(item)
                with pool.Fori(0, BODIES) as it:
                    def low(s):
                        off = unit(s)[3]
                        pool.wait_ge(pv_done, it * UNITS + after(s - 2))
                        pool.wait_ge(p_hi_ready, it * UNITS + after(s))
                        pool.tensor_tensor(p_lo[s % 2][:, off:], p[s % 2][:, off:], p_hi[s % 2][:, off:].bitcast(F32),
                                           ALU.subtract).then_inc(p_lo_ready, 1)

                    def gdn(j, k, a):
                        n = it * CHUNKS + j
                        m = n * 2 + a
                        par = j % 2
                        mine = slice(a * SH, (a + 1) * SH)
                        H2 = [P, SH, P]

                        def level(i):
                            b = 1 << i
                            mask = halves(masks[:, i, :], b, 1).unsqueeze(1).broadcast_to([P, SH, P // (2 * b), b])
                            pool.tensor_tensor(halves(C[i][:, mine, :], b, 1), halves(LT[:, mine, :], b, 1), mask, ALU.mult)\
                                .then_inc(C_ready, 1)

                        if k == SS:
                            pool.wait_ge(g_landed[par], it * 128 + (64 * (j // 2) + 64))
                            pool.wait_ge(cc_ready, n + after(0))
                            pool.wait_ge(LT_ready, m + after(-2))
                            pool.wait_ge(intra_ready, m + after(-2))
                            pool.tensor_tensor(DT[:, mine, :], grow[par][:, mine, :],
                                               wide(cc[:, 2 * GH + a * SH:2 * GH + (a + 1) * SH], P), ALU.subtract)\
                                .then_inc(dd0_ready, 1)
                            pool.wait_ge(dd0_ready, m + after(0))
                            pool.tensor_tensor(DT[:, mine, :], DT[:, mine, :], masks[:, LEVELS + 2:, :].broadcast_to(H2),
                                               ALU.add).then_inc(dd_ready, 1)
                            pool.wait_ge(kk_ready, m + after(0))
                            pool.tensor_tensor(rk[a][:], kk[a][:], half[:], ALU.pow).then_inc(rk_ready, 1)
                        elif k == TVK:
                            pool.wait_ge(DT_ready, m + after(0))
                            pool.tensor_tensor(DTb[:, mine, :], DT[:, mine, :], brow[par][:, mine, :], ALU.mult)\
                                .then_inc(DTb_ready, 1)
                            pool.wait_ge(eg_ready, m + after(0))
                            pool.tensor_tensor(qg[:, mine, :], cin[par][:, mine, :], eg[:, mine, :], ALU.mult)\
                                .then_inc(qg_ready, 1)
                        elif k == TKN:
                            pool.wait_ge(kn_ready, m + after(0))
                            pool.tensor_tensor(kend[:, mine, :], kn[:, mine, :], DT[:, mine, P - 1:].broadcast_to(H2),
                                               ALU.mult).then_inc(kend_ready, 1)
                        elif k == GQ:
                            pool.wait_ge(LT_ready, m + after(0))
                            level(0)
                            level(1)
                            pool.wait_ge(C_ready, level_at(n, 0, a) + after(0))
                            pool.tensor_tensor(XT[:, mine, :], C[0][:, mine, :], ident4[:, 0:SH, :], ALU.add)\
                                .then_inc(XT0_ready, 1)
                        elif TX <= k < TX + LEVELS - 1:
                            level(k - TX + 2)
                        elif k == SUMS:
                            pool.wait_ge(mo_ready, m + after(0))
                            pool.tensor_tensor(ro[a][:], so[a][:], half[:], ALU.pow).then_inc(ro_ready, 1)

                    for s in range(SLOTS):
                        for q in range(PLACES):
                            for item in AUX_AT[s][q]:
                                do_aux(item, it)
                            for j, k, a in gdn_at(s, q):
                                gdn(j, k, a)
                            if q == 0 and 1 <= s <= UNITS:
                                low(s - 1)

            @block.vector
            def _(dve):
                credit(dve, [aux_used, mcol_ready, row_ready, p_hi_ready, den_ready, rcol_ready, gated_ready, yb_ready,
                             v_hi_ready, cc_ready, kk_ready, kn_ready, LT_ready, intra_ready, XT_ready, R2_ready,
                             so_ready, mo_ready, on_ready, S_ready, ya_ready])
                dve.memset(over_q[:, P:], NEG)
                dve.memset(over_k[:, 0:P], NEG).then_inc(consts_split, 2)
                dve.wait_ge(consts_landed, 48)
                dve.tensor_copy(ident_b[:], ident[:]).then_inc(consts_split, 1)
                dve.tensor_copy(over_q[:, 0:P], masks[:, LEVELS + 1, :]).then_inc(consts_split, 1)
                dve.tensor_copy(over_k[:, P:], masks[:, LEVELS + 2, :]).then_inc(consts_split, 1)
                dve.tensor_scalar(half_w[:], norm_w[:], 0.5, None, ALU.mult).then_inc(half_w_ready, 1)
                for q, b in enumerate((aux[0], aux[1], st[0], st[1])):
                    dve.wait_ge(cols_in_psum, q + 1)
                    dve.tensor_copy(cols[:, 4 * q:4 * q + 4, :], b[:].rearrange("p (c r) -> p c r", c=4)[:, :, 0:GATES])\
                       .then_inc(cols_ready, 1)
                dve.wait_ge(cols_ready, 4)
                dve.tensor_scalar(gcol[:, :, 0:GH], cols[:, :, BETA:BETA + GH], 0.5, None, ALU.mult)
                dve.tensor_copy(gcol[:, :, 2 * GH:], cols[:, :, DECAY:DECAY + GH])
                dve.tensor_scalar(fcol[:].rearrange("p h c -> p c h"), cols[:, :, FORGET:FORGET + FH], -1.0, None, ALU.mult)\
                   .then_inc(gcol_ready, 1)
                dve.wait_ge(beta_exp_ready, 1)
                dve.scalar_tensor_tensor(gcol[:, :, GH:2 * GH], gcol[:, :, GH:2 * GH], -1.0, cols[:, :, BETA:BETA + GH],
                                         ALU.mult, ALU.mult).then_inc(gcol_ready, 1)
                dve.wait_ge(gcol_ready, 2)
                dve.wait_ge(half_w_ready, 1)
                dve.wait_ge(zeros_set, 1)
                dve.wait_ge(rows_set, 2)

                def do_aux(item, it=0):
                    kind, *what = item
                    m = AUX_INDEX[item]
                    b = aux[m % 2]

                    def came():
                        dve.wait_ge(aux_ready, it * len(AUX) + after(m))

                    if kind == "v":
                        cut = slice(what[0] * 4, what[0] * 4 + 4)
                        src = b[:].rearrange("p (c h d) -> p c h d", c=4, h=2)
                        if what[0] == 0:
                            dve.wait_ge(pv_done, it * UNITS + after(-1))
                        came()
                        dve.tensor_copy(v_hi[:, cut, :, 0:FD], src).then_inc(v_hi_ready, 1)
                        dve.wait_ge(v_hi_ready, it * 4 + after(what[0]))
                        dve.tensor_tensor(v_lo[:, cut, :, :], src, v_hi[:, cut, :, 0:FD].bitcast(F32), ALU.subtract)\
                           .then_inc(aux_used, 1)
                    elif kind == "max":
                        hp, g, a, kb4 = what
                        G = hp * NB + g
                        n = max(a + 1, 2) * P if kb4 == g else 512
                        if a == 0 and kb4 == 0:
                            dve.wait_ge(mcol_ready, it * GROUPS + after(G - 1))
                        came()
                        dve.reduce_max(maxima[:, a, kb4:kb4 + 1], b[:, 0:n], AX.X).then_inc(aux_used, 1)
                        if a == 3 and kb4 == g:
                            dve.wait_ge(aux_used, it * len(AUX) + after(m))
                            dve.wait_ge(max_diag_ready, it * GROUPS + after(G - 1))
                            dve.reduce_max(mcol[:], maxima[:, :, 0:g + 1], AX.X).then_inc(mcol_ready, 1)
                    elif kind == "row":
                        hp, g = what
                        G = hp * NB + g
                        dve.wait_ge(yb_ready, it * GROUPS + after(G - 4))
                        came()
                        dve.tensor_scalar(Q2[G % 4][FD:FD + 1, :], b[0:1, :], -1.0, None, ALU.mult).then_inc(row_ready, 1)
                        dve.wait_ge(row_ready, it * GROUPS + after(G))
                        dve.sem_inc(aux_used, 1)
                    elif kind == "sum":
                        hp, g = what
                        G = hp * NB + g
                        dve.wait_ge(rec_diag_ready, it * GROUPS + after(G - 1))
                        came()
                        dve.reciprocal(rcol[:], b[:, 0:4]).then_inc(rcol_ready, 1)
                        dve.wait_ge(rcol_ready, it * GROUPS + after(G))
                        dve.sem_inc(aux_used, 1)
                    else:
                        hp, g = what
                        G = hp * NB + g
                        dve.wait_ge(yb_stored[G % 2], it * (16 * GROUPS // 2) + (16 + 16 * (G // 2)))
                        came()
                        dve.scalar_tensor_tensor(yb[G % 2][:], gated[:], 0.5, b[0:FD, :], ALU.mult, ALU.mult)\
                           .then_inc(yb_ready, 1)
                        dve.wait_ge(yb_ready, it * GROUPS + after(G))
                        dve.sem_inc(aux_used, 1)

                for item in FIRST_AUX:
                    do_aux(item)
                with dve.Fori(0, BODIES) as it:
                    def finish(hp, g):
                        G = hp * NB + g
                        dve.wait_ge(pv_done, it * UNITS + after(hp * len(HEAD_UNITS) + HEAD_UNITS.index((g, 4 * g + 3))))
                        dve.tensor_copy(den[:], pv[G % 2][FD:FD + 1, :]).then_inc(den_ready, 1)
                        dve.wait_ge(zb_landed[G % 2], it * 64 + (16 * (G // 2) + 16))
                        dve.wait_ge(yb_ready, it * GROUPS + after(G - 1))
                        dve.wait_ge(den_ready, it * GROUPS + after(G))
                        dve.tensor_tensor(gated[:], pv[G % 2][0:FD, :], zb[G % 2][:], ALU.mult).then_inc(gated_ready, 1)

                    def high(s):
                        off = unit(s)[3]
                        dve.wait_ge(pv_done, it * UNITS + after(s - 2))
                        dve.wait_ge(p_ready, it * UNITS + after(s))
                        dve.tensor_copy(p_hi[s % 2][:, off:], p[s % 2][:, off:]).then_inc(p_hi_ready, 1)

                    def gdn(j, k, a):
                        n = it * CHUNKS + j
                        m = n * 2 + a
                        par = j % 2
                        mine = slice(a * SH, (a + 1) * SH)
                        b = gd4[a][:, 0:SH, :]
                        b2 = gd4[a][:, SH:, :]

                        def came():
                            dve.wait_ge(g_step, step_at(n, k, a))

                        if k == SS:
                            if a == 0:
                                dve.wait_ge(ya_ready, m + after(-1))
                                dve.wait_ge(dd0_ready, m + after(-1))
                                dve.tensor_copy(cc[:], gcol[:, n, :]).then_inc(cc_ready, 1)
                            came()
                            dve.wait_ge(rk_ready, m + after(-2))
                            dve.tensor_scalar(qe[a][:], gd[a][:, 0:SH], GD * NORM_EPS, 4 * GD * NORM_EPS ** 2,
                                              ALU.mult, ALU.add)
                            dve.tensor_scalar(kk[a][:], gd[a][:, SH:2 * SH], 4 * NORM_EPS, None, ALU.add).then_inc(kk_ready, 1)
                        elif k == TVK:
                            dve.wait_ge(cc_ready, n + after(0))
                            came()
                            dve.tensor_tensor(vb[:, mine, :], b, wide(cc[:, mine], P), ALU.mult)
                            dve.wait_ge(kend_ready, m + after(-2))
                            dve.wait_ge(rk_ready, m + after(0))
                            dve.tensor_tensor(kn[:, mine, :], b2, wide(rk[a][:], P), ALU.mult).then_inc(kn_ready, 1)
                        elif k == GQ:
                            dve.wait_ge(DTb_ready, m + after(0))
                            dve.wait_ge(C_ready, level_at(n, 0, 0) + after(-1))
                            came()
                            dve.scalar_tensor_tensor(LT[:, mine, :], b, -1.0, DTb[:, mine, :], ALU.mult, ALU.mult)\
                               .then_inc(LT_ready, 1)
                            dve.tensor_tensor(intra[:, mine, :], b2, DT[:, mine, :], ALU.mult).then_inc(intra_ready, 1)
                        elif LEVEL <= k < KS and (k - LEVEL) % 2:
                            lv = (k - LEVEL) // 2
                            width = 2 << lv
                            if lv == 0:
                                dve.wait_ge(X0_ready, m + after(0))
                            else:
                                dve.wait_ge(XT_ready, n * (2 * LEVELS) + (2 * (lv - 1) + a) + after(0))
                            came()
                            if lv < LEVELS - 1:
                                even = halves(X[:, mine, :], width, 0)
                                dve.tensor_tensor(even, even, blocks(gd8[a][:, 0:SH, :], width), ALU.add)
                            odd = halves(XT[:, mine, :], width, 1)
                            dve.tensor_tensor(odd, odd, blocks(gd8[a][:, SH:2 * SH, :], width), ALU.add).then_inc(XT_ready, 1)
                        elif k == KS:
                            came()
                            for i in range(SH):
                                h = a * SH + i
                                last = dve.scalar_tensor_tensor(R2[:, h, :], b[:, i, :], cc[:, GH + h:GH + h + 1],
                                                                vb[:, h, :], ALU.mult, ALU.add)
                            last.then_inc(R2_ready, 1)
                        elif k == OD:
                            came()
                            for i in range(SH):
                                h = a * SH + i
                                last = dve.scalar_tensor_tensor(S[:, h, :], S[:, h, :], eg[:, h, P - 1:P], b2[:, i, :],
                                                                ALU.mult, ALU.add)
                            last.then_inc(S_ready, 1)
                        elif k == SUMS:
                            dve.wait_ge(sqo_ready, m + after(0))
                            dve.wait_ge(ro_ready, m + after(-2))
                            dve.reduce_sum(so[a][:], sq[:, mine, :], AX.X).then_inc(so_ready, 1)
                            dve.wait_ge(so_ready, m + after(0))
                            dve.scalar_tensor_tensor(so[a][:], so[a][:], 1.0 / GD, qe[a][:], ALU.mult, ALU.add)\
                               .then_inc(mo_ready, 1)
                        elif k == NORM:
                            dve.wait_ge(ro_ready, m + after(0))
                            dve.tensor_tensor(on[:, mine, :], b, wide(ro[a][:], P), ALU.mult).then_inc(on_ready, 1)
                        elif k == TY:
                            dve.wait_ge(ya_stored[par], it * 32 + (16 * (j // 2) + 16))
                            came()
                            dve.scalar_tensor_tensor(ya[par][:, mine, :], b, half_w[:], za[par][:, mine, :],
                                                     ALU.mult, ALU.mult).then_inc(ya_ready, 1)

                    for s in range(SLOTS):
                        if 1 <= s <= UNITS:
                            high(s - 1)
                        if s < UNITS and s % len(HEAD_UNITS) == 0:
                            hp = s // len(HEAD_UNITS)
                            dve.wait_ge(p_ready, it * UNITS + after(s - 1))
                            dve.tensor_copy(fbias[hp][:], fcol[:, it * 2 + hp, :]).then_inc(fbias_ready, 1)
                        for q in range(PLACES):
                            if q == 2:
                                for kind, *what in AUX_AT[s][q]:
                                    if kind == "sum":
                                        finish(*what)
                            for item in AUX_AT[s][q]:
                                do_aux(item, it)
                            for j, k, a in gdn_at(s, q):
                                gdn(j, k, a)


def project_out(nc, io, scr, out):
    TILES = SEQ // P
    with ExitStack() as ctx:
        def sb(name, shape, dt=F32):
            return ctx.enter_context(nc.sbuf_tensor("o_" + name, shape, dt))

        def sem(name):
            return ctx.enter_context(nc.semaphore("o_" + name))

        w_raw = [sb(f"w_raw{i}", [P, D_MODEL]) for i in range(2)]
        w_hi = sb("w_hi", [P, KT, D_MODEL], F32R)
        w_lo = sb("w_lo", [P, KT, D_MODEL], F32R)
        ln_g, ln_b = sb("ln_g", [P, D_MODEL]), sb("ln_b", [P, D_MODEL])
        y = [sb(f"y{i}", [P, KT, P]) for i in range(2)]
        y_hi = [sb(f"y_hi{i}", [P, KT, P], F32R) for i in range(2)]
        y_lo = [sb(f"y_lo{i}", [P, KT, P], F32R) for i in range(2)]
        x = [sb(f"x{i}", [P, D_MODEL]) for i in range(2)]
        h = [sb(f"h{i}", [P, D_MODEL]) for i in range(2)]
        scaled = [sb(f"scaled{i}", [P, D_MODEL]) for i in range(2)]
        res = [sb(f"res{i}", [P, D_MODEL]) for i in range(2)]
        stats = sb("stats", [P, 2, 6])
        mv = sb("mv", [P, 2])
        rstd0, rstd = sb("rstd0", [P, 1]), sb("rstd", [P, 1])
        half = sb("half", [P, 1])
        banks = [ctx.enter_context(nc.psum_tensor(f"o_bank{i}", [P, D_MODEL], F32)) for i in range(2)]

        w_landed = [sem(f"w_landed{i}") for i in range(2)]
        w_hi_ready, w_split = sem("w_hi_ready"), sem("w_split")
        ln_landed = sem("ln_landed")
        y_landed = [sem(f"y_landed{i}") for i in range(2)]
        x_landed = [sem(f"x_landed{i}") for i in range(2)]
        half_set = sem("half_set")
        mv_free = sem("mv_free")
        y_hi_ready, y_lo_ready, summed, h_ready = sem("y_hi_ready"), sem("y_lo_ready"), sem("summed"), sem("h_ready")
        stats_ready, mv_ready, var_ready, rstd_ready = (
            sem("stats_ready"), sem("mv_ready"), sem("var_ready"), sem("rstd_ready"))
        normed, scaled_ready, res_ready = sem("normed"), sem("scaled_ready"), sem("res_ready")
        stored = [sem(f"stored{i}") for i in range(2)]
        mixed = scr["mixT"].rearrange("k p (n t) -> n p k t", t=P)
        x_rows = io["x"].rearrange("(n t) d -> n t d", t=P)
        out_rows = out.rearrange("(n t) d -> n t d", t=P)

        with nc.Block() as block:
            @block.sync
            def _(sp):
                for i in range(2):
                    sp.sem_inc(stored[i], 16)

                def load(t, par, first=False):
                    if not first:
                        sp.wait_ge(y_lo_ready, t + after(-2))
                    sp.dma_start(y[par][:], mixed[t]).then_inc(y_landed[par], 16)
                    if not first:
                        sp.wait_ge(h_ready, t + after(-2))
                    sp.dma_start(x[par][:], x_rows[t]).then_inc(x_landed[par], 16)

                load(0, 0, first=True)
                for k in range(KT):
                    if k >= 2:
                        sp.wait_ge(w_split, k - 1)
                    sp.dma_start(w_raw[k % 2][:], io["w_out"][k]).then_inc(w_landed[k % 2], 16)
                load(1, 1, first=True)
                sp.dma_start(ln_g[:], io["ln_g"].broadcast_to([P, D_MODEL])).then_inc(ln_landed, 16)
                sp.dma_start(ln_b[:], io["ln_b"].broadcast_to([P, D_MODEL])).then_inc(ln_landed, 16)

                def store(t, par):
                    sp.wait_ge(res_ready, t + after(0))
                    sp.dma_start(out_rows[t], res[par][:]).then_inc(stored[par], 16)

                with sp.Fori(0, TILES // 2 - 1) as i:
                    for par in range(2):
                        load(i * 2 + (2 + par), par)
                        store(i * 2 + par, par)
                for par in range(2):
                    store(TILES - 2 + par, par)
                for par in range(2):
                    sp.wait_ge(stored[par], 16 + 16 * TILES // 2)

            @block.gpsimd
            def _(pool):
                credit(pool, [rstd_ready, scaled_ready])
                pool.memset(half[:], -0.5).then_inc(half_set, 1)
                pool.wait_ge(half_set, 1)
                pool.wait_ge(ln_landed, 32)
                with pool.Fori(0, TILES // 2) as i:
                    for par in range(2):
                        t = i * 2 + par
                        pool.wait_ge(var_ready, t + after(0))
                        pool.tensor_tensor(rstd[:], rstd0[:], half[:], ALU.pow).then_inc(rstd_ready, 1)
                        pool.wait_ge(normed, t + after(0))
                        pool.wait_ge(res_ready, t + after(-2))
                        pool.tensor_tensor(scaled[par][:], h[par][:], ln_g[:], ALU.mult).then_inc(scaled_ready, 1)

            @block.tensor
            def _(pe):
                credit(pe, [summed])

                def tile(t, par):
                    pe.wait_ge(h_ready, t + after(-2))
                    for k in range(KT):
                        if isinstance(t, int) and t == 0:
                            pe.wait_ge(w_split, k + 1)
                        if k == 0:
                            pe.wait_ge(y_lo_ready, t + after(0))
                        for n, (a, b) in enumerate(((y_hi, w_hi), (y_hi, w_lo), (y_lo, w_hi))):
                            for c in range(D_MODEL // 512):
                                cut = slice(c * 512, (c + 1) * 512)
                                mm = pe.matmul(banks[par][:, cut], a[par][:, k, :], b[:, k, cut],
                                               start=(k == 0 and n == 0), stop=(k == KT - 1 and n == 2))
                    mm.then_inc(summed, 1)

                tile(0, 0)
                tile(1, 1)
                with pe.Fori(1, TILES // 2) as i:
                    for par in range(2):
                        tile(i * 2 + par, par)

            @block.scalar
            def _(act):
                credit(act, [y_hi_ready])
                for k in range(KT):
                    act.wait_ge(w_landed[k % 2], 16 * (k // 2 + 1))
                    if k == 1:
                        act.wait_ge(y_landed[0], 16)
                        act.activation(y_hi[0][:], y[0][:], ACT.Copy).then_inc(y_hi_ready, 1)
                    act.activation(w_hi[:, k, :], w_raw[k % 2][:], ACT.Copy).then_inc(w_hi_ready, 1)

                def hi(t, par, landed):
                    act.wait_ge(y_landed[par], landed)
                    act.wait_ge(summed, t + after(-2))
                    act.activation(y_hi[par][:], y[par][:], ACT.Copy).then_inc(y_hi_ready, 1)

                hi(1, 1, 16)
                with act.Fori(1, TILES // 2) as i:
                    for par in range(2):
                        hi(i * 2 + par, par, i * 16 + 16)

            @block.vector
            def _(dve):
                credit(dve, [y_lo_ready, h_ready, stats_ready, mv_ready, var_ready, normed, res_ready])

                def lo(t, par):
                    dve.wait_ge(y_hi_ready, t + after(0))
                    dve.wait_ge(summed, t + after(-2))
                    dve.tensor_tensor(y_lo[par][:], y[par][:], y_hi[par][:].bitcast(F32), ALU.subtract)\
                       .then_inc(y_lo_ready, 1)

                for k in range(KT):
                    dve.wait_ge(w_hi_ready, k + 1)
                    if k == 1:
                        lo(0, 0)
                    dve.tensor_tensor(w_lo[:, k, :], w_raw[k % 2][:], w_hi[:, k, :].bitcast(F32), ALU.subtract)\
                       .then_inc(w_split, 1)
                lo(1, 1)

                def norm(t, par, landed):
                    dve.wait_ge(x_landed[par], landed)
                    dve.wait_ge(summed, t + after(0))
                    dve.wait_ge(scaled_ready, t + after(-2))
                    dve.scalar_tensor_tensor(h[par][:], x[par][:], DEEP_ALPHA, banks[par][:], ALU.mult, ALU.add)\
                       .then_inc(h_ready, 1)
                    dve.wait_ge(h_ready, t + after(0))
                    dve.wait_ge(mv_ready, t + after(-1))
                    dve.bn_stats(stats[:, 0, :], h[par][:, 0:512])
                    dve.bn_stats(stats[:, 1, :], h[par][:, 512:]).then_inc(stats_ready, 1)
                    dve.wait_ge(stats_ready, t + after(0))
                    dve.wait_ge(normed, t + after(-1))
                    dve.sem_inc(mv_free, 1)
                    dve.bn_aggr(mv[:], stats[:]).then_inc(mv_ready, 1)
                    dve.wait_ge(mv_ready, t + after(0))
                    dve.wait_ge(rstd_ready, t + after(-1))
                    dve.tensor_scalar(rstd0[:], mv[:, 1:2], LN_EPS, None, ALU.add).then_inc(var_ready, 1)

                def finish(t, par, stored_value):
                    dve.wait_ge(rstd_ready, t + after(0))
                    dve.tensor_scalar(h[par][:], h[par][:], mv[:, 0:1], rstd[:], ALU.subtract, ALU.mult)\
                       .then_inc(normed, 1)
                    dve.wait_ge(scaled_ready, t + after(0))
                    dve.wait_ge(stored[par], stored_value)
                    dve.tensor_tensor(res[par][:], scaled[par][:], ln_b[:], ALU.add).then_inc(res_ready, 1)

                dve.wait_ge(ln_landed, 32)
                with dve.Fori(0, TILES // 2 - 1) as i:
                    for par in range(2):
                        norm(i * 2 + par, par, i * 16 + 16)
                        lo(i * 2 + (par + 2), par)
                        finish(i * 2 + par, par, i * 16 + 16)
                for par in range(2):
                    t = TILES - 2 + par
                    norm(t, par, 16 * TILES // 2)
                    finish(t, par, 16 * TILES // 2)




def build(nc, io, out):
    def scratch(name, shape, dt=F32):
        return nc.dram_tensor("dram_" + name, shape, dt).ap()

    scr = {
        "feat": scratch("feat", (N_FEAT, P, SEQ)),
        "gates": scratch("gates", (GATES, SEQ)),
        "neg_cum": scratch("neg_cum", (FH, SEQ)),
        "mixT": scratch("mixT", (KT, P, SEQ)),
    }
    for n in ("q_hi", "q_lo", "k_hi", "k_lo"):
        scr[n] = scratch(n, (4, P, SEQ))
    project(nc, io, scr)
    mix(nc, io, scr)
    project_out(nc, io, scr, out)


def tiles_of(w, columns):
    return w[:, columns].reshape(KT, P, P).transpose(1, 0, 2).reshape(P, KT * P)


def constants():
    s, c = np.arange(P)[:, None], np.arange(P)[None, :]
    levels = [((s // (2 * b) == c // (2 * b)) & (s // b % 2 == 0) & (c // b % 2 == 1)).astype(np.float32)
              for b in (1, 2, 4, 8, 16, 32, 64)]
    neg = np.float32(NEG)
    return (np.stack(levels + [np.where(c > s, neg, np.float32(0)), np.where(c < s, neg, np.float32(0))], 1),
            np.eye(P, dtype=np.float32))


def kernel(x, w_in, conv_w, a_log, dt_bias, gdn_norm_w, fox_f_bias, w_out, ln_g, ln_b):
    import concourse.bacc as bacc
    from concourse.bass_utils import run_bass_kernel_spmd as run

    GW, FW = GH * GD, FH * FD
    w = np.asarray(w_in)[0]
    beta_at = 4 * GW
    qb_at = beta_at + 2 * GH
    gates = np.zeros((D_MODEL, P), w.dtype)
    gates[:, BETA:BETA + GH] = w[:, beta_at:beta_at + GH]
    gates[:, DECAY:DECAY + GH] = w[:, beta_at + GH:qb_at]
    gates[:, FORGET:FORGET + FH] = w[:, qb_at + 4 * FW:]
    starts = [i * P for i in range(16)] + [qb_at + 3 * FW + i * P for i in range(4)]
    for i in range(4):
        starts += [qb_at + i * P, qb_at + FW + i * P]
    starts += [qb_at + 2 * FW + i * P for i in range(4)]
    masks, ident = constants()
    arrays = {
        "masks": masks,
        "ident": ident,
        "w": np.stack([tiles_of(gates, slice(0, P))] + [tiles_of(w, slice(s, s + P)) for s in starts]),
        "xT": np.ascontiguousarray(np.asarray(x)[0].T.reshape(KT, P, SEQ)),
        "x": np.ascontiguousarray(np.asarray(x)[0]),
        "taps": np.ascontiguousarray(np.asarray(conv_w)[0].reshape(CONV_K, 12, P).transpose(2, 1, 0)),
        "dt_bias": np.asarray(dt_bias).reshape(GH, 1),
        "a_log": np.asarray(a_log).reshape(GH, 1),
        "f_bias": np.asarray(fox_f_bias).reshape(FH, 1),
        "norm_w": np.asarray(gdn_norm_w).reshape(GD, 1),
        "w_out": np.ascontiguousarray(np.asarray(w_out)[0].reshape(KT, P, D_MODEL)),
        "ln_g": np.asarray(ln_g).reshape(1, D_MODEL),
        "ln_b": np.asarray(ln_b).reshape(1, D_MODEL),
    }
    nc = bacc.Bacc("TRN2", target_bir_lowering=False, num_devices=1)
    io = {n: nc.dram_tensor("in_" + n, a.shape, F32, kind="ExternalInput").ap() for n, a in arrays.items()}
    out = nc.dram_tensor("out", (SEQ, D_MODEL), F32, kind="ExternalOutput").ap()
    build(nc, io, out)
    r = run(nc, [{"in_" + n: a for n, a in arrays.items()}], core_ids=[0])
    return r.results[0]["out"].reshape(1, SEQ, D_MODEL)
```

```python
from contextlib import ExitStack

import numpy as np

import concourse.bass as bass
from concourse import mybir

F32 = mybir.dt.float32
F32R = mybir.dt.float32r
BF16 = mybir.dt.bfloat16
ALU = mybir.AluOpType
ACT = mybir.ActivationFunctionType
AX = mybir.AxisListType

P = 128
SEQ = 2048
D_MODEL = 1024
KT = D_MODEL // P
CHUNK = P
NCH = SEQ // CHUNK
NB = SEQ // 512
GH, GD = 4, 128
FH, FD = 8, 64
CONV_K = 4
DEEP_ALPHA = 2.0 ** 0.25
LN_EPS = 1e-5
NORM_EPS = 1e-6
NEG = -1.0e30

BETA, DECAY, FORGET, GATES = 0, 32, 64, 72
CONV_T, ZA_T, ZB_T, VB_T = 0, 12, 16, 20
N_FEAT = 24

CREDIT = 4


def after(n):
    return n + (CREDIT + 1)


def credit(eng, sems):
    for s in sems:
        eng.sem_inc(s, CREDIT)


def flat(ap):
    return ap.rearrange("p a b -> p (a b)")


def wide(cols, n):
    return cols.unsqueeze(2).broadcast_to([cols.shape[0], cols.shape[1], n])


def project(nc, io, scr):
    PAD = 4
    CONV_AT, Z_AT, QK_AT, V_AT, TILES = 1, 13, 21, 29, 33
    with ExitStack() as ctx:
        def sb(name, shape, dt=F32):
            return ctx.enter_context(nc.sbuf_tensor(name, shape, dt))

        def sem(name):
            return ctx.enter_context(nc.semaphore(name))

        x_hi = sb("x_hi", [P, KT, SEQ], F32R)
        x_lo = sb("x_lo", [P, KT, SEQ], F32R)
        w_raw = sb("w_raw", [P, 2, KT * P])
        w_hi = sb("w_hi", [P, 2, KT * P], F32R)
        w_lo = sb("w_lo", [P, 2, KT * P], F32R)
        u = sb("conv_in", [P, PAD + SEQ])
        acc = sb("conv_acc", [P, SEQ])
        res = [sb(f"result{i}", [P, SEQ]) for i in range(2)]
        hi = sb("qk_hi", [P, SEQ], F32R)
        lo = sb("qk_lo", [P, SEQ], F32R)
        taps = sb("taps", [P, 12, CONV_K])
        tap = sb("tap", [P, CONV_K])
        gate_bias = sb("gate_bias", [GATES, 1])
        gate_sign = sb("gate_sign", [GATES, 1])
        gate_mult = sb("gate_mult", [GATES, 1])
        banks = [ctx.enter_context(nc.psum_tensor(f"proj{i}", [P, SEQ], F32)) for i in range(2)]

        x_landed = [sem(f"x_landed{i}") for i in range(2)]
        x_hi_ready = sem("x_hi_ready")
        x_split = sem("x_split")
        taps_landed = sem("taps_landed")
        gate_consts_landed = sem("gate_consts_landed")
        gate_consts_set = sem("gate_consts_set")
        pad_set = sem("pad_set")
        w_landed = [sem(f"w_landed{i}") for i in range(2)]
        pair_free = sem("pair_free")
        w_hi_ready = sem("w_hi_ready")
        w_split = sem("w_split")
        projected = sem("projected")
        bank_read = sem("bank_read")
        u_ready = sem("u_ready")
        conv_step = sem("conv_step")
        conv_ready = sem("conv_ready")
        tanh_ready = sem("tanh_ready")
        result_ready = sem("result_ready")
        hi_ready = sem("hi_ready")
        lo_ready = sem("lo_ready")
        stored = [sem(f"stored{i}") for i in range(2)]
        qk_stored = sem("qk_stored")
        gates_stored = sem("gates_stored")
        gate_mult_ready = sem("gate_mult_ready")
        gate_y_abs = sem("gate_y_abs")
        gate_exp = sem("gate_exp")
        gate_ln = sem("gate_ln")
        gate_log = sem("gate_log")
        gate_log_scaled = sem("gate_log_scaled")
        scan_mask_set = sem("scan_mask_set")
        gate_cum = sem("gate_cum")
        neg_cum_ready = sem("neg_cum_ready")
        beta_ready = sem("beta_ready")

        with nc.Block() as block:
            @block.sync
            def _(sp):
                for par in range(2):
                    sp.sem_inc(stored[par], 16)
                sp.sem_inc(qk_stored, 32)
                for t in range(2):
                    sp.dma_start(w_raw[:, t, :], io["w"][t]).then_inc(w_landed[t], 16)
                for k in range(KT):
                    if k >= 2:
                        sp.wait_ge(x_split, k - 1)
                    sp.dma_start(res[k % 2][:], io["xT"][k]).then_inc(x_landed[k % 2], 16)
                    if k == 1:
                        sp.dma_start(taps[:], io["taps"]).then_inc(taps_landed, 16)
                        sp.wait_ge(gate_consts_set, 1)
                        sp.dma_start(gate_bias[DECAY:DECAY + GH, :], io["dt_bias"]).then_inc(gate_consts_landed, 16)
                        sp.dma_start(gate_bias[FORGET:FORGET + FH, :], io["f_bias"]).then_inc(gate_consts_landed, 16)
                        sp.dma_start(gate_mult[DECAY:DECAY + GH, :], io["a_log"]).then_inc(gate_consts_landed, 16)

                def load_w(t, par):
                    sp.wait_ge(w_split, t - 1)
                    sp.dma_start(w_raw[:, par, :], io["w"][t]).then_inc(w_landed[par], 16)

                load_w(2, 0)
                sp.wait_ge(neg_cum_ready, 1)
                sp.dma_start(scr["neg_cum"], hi[FORGET:FORGET + FH, :].bitcast(F32)).then_inc(gates_stored, 16)
                sp.wait_ge(beta_ready, 1)
                sp.dma_start(scr["gates"], res[0][0:GATES, :]).then_inc(gates_stored, 16)

                def store_results(pairs, first, n_before, place):
                    with sp.Fori(0, pairs) as i:
                        for j in range(2):
                            par = (first + j) % 2
                            load_w(i * 2 + (first + j + 2), par)
                            sp.wait_ge(result_ready, i * 2 + after(n_before + j))
                            sp.dma_start(scr["feat"][i * 2 + (place + j)], res[par][:]).then_inc(stored[par], 16)

                store_results(6, CONV_AT, 0, CONV_T)
                store_results(4, Z_AT, 12, ZA_T)
                with sp.Fori(0, 4) as i:
                    for j, (h, l) in enumerate((("q_hi", "q_lo"), ("k_hi", "k_lo"))):
                        load_w(i * 2 + (QK_AT + j + 2), (QK_AT + j) % 2)
                        sp.wait_ge(hi_ready, i * 2 + after(j))
                        sp.dma_start(scr[h][i], hi[:].bitcast(F32)).then_inc(qk_stored, 16)
                        sp.wait_ge(lo_ready, i * 2 + after(j))
                        sp.dma_start(scr[l][i], lo[:].bitcast(F32)).then_inc(qk_stored, 16)
                for j in range(4):
                    t = V_AT + j
                    if t + 2 < TILES:
                        load_w(t + 2, t % 2)
                    sp.wait_ge(result_ready, after(20 + j))
                    sp.dma_start(scr["feat"][VB_T + j], res[t % 2][:]).then_inc(stored[t % 2], 16)
                sp.wait_ge(gates_stored, 32)
                sp.wait_ge(qk_stored, 32 + 16 * 16)
                for par in range(2):
                    sp.wait_ge(stored[par], 16 + 16 * 12)

            @block.gpsimd
            def _(pool):
                credit(pool, [w_hi_ready])
                pool.memset(gate_bias[:], 0.0)
                pool.memset(gate_sign[:], 1.0)
                pool.memset(u[:, 0:PAD], 0.0).then_inc(pad_set, 1)
                pool.memset(gate_mult[:], 1.0).then_inc(gate_consts_set, 1)
                pool.wait_ge(gate_consts_set, 1)
                pool.memset(gate_sign[DECAY:DECAY + 32, :], -1.0).then_inc(gate_consts_set, 1)
                pool.wait_ge(gate_consts_set, 2)

                def split(t, par, landed):
                    pool.wait_ge(w_landed[par], landed)
                    if not isinstance(t, int) or t >= 2:
                        pool.wait_ge(projected, t - 1)
                    pool.sem_inc(pair_free, 1)
                    pool.tensor_copy(w_hi[:, par, :], w_raw[:, par, :]).then_inc(w_hi_ready, 1)
                    pool.wait_ge(w_hi_ready, t + after(0))
                    pool.tensor_tensor(w_lo[:, par, :], w_raw[:, par, :], w_hi[:, par, :].bitcast(F32),
                                       ALU.subtract).then_inc(w_split, 1)

                split(0, 0, 16)
                split(1, 1, 16)
                split(2, 0, 32)
                with pool.Fori(0, (TILES - 3) // 2) as i:
                    split(i * 2 + 3, 1, i * 16 + 32)
                    split(i * 2 + 4, 0, i * 16 + 48)

            @block.tensor
            def _(pe):
                def tile(t, par):
                    pe.wait_ge(w_split, t + 1)
                    first = isinstance(t, int)
                    if not first:
                        pe.wait_ge(bank_read, t + (CREDIT - 1))
                    for k in range(KT):
                        if first:
                            pe.wait_ge(x_split, k + 1)
                        for n, (w, x) in enumerate(((w_hi, x_hi), (w_hi, x_lo), (w_lo, x_hi))):
                            for b in range(NB):
                                mm = pe.matmul(banks[par][:, b * 512:(b + 1) * 512], w[:, par, k * P:(k + 1) * P],
                                               x[:, k, b * 512:(b + 1) * 512],
                                               start=(k == 0 and n == 0), stop=(k == KT - 1 and n == 2))
                    mm.then_inc(projected, 1)

                tile(0, 0)
                with pe.Fori(0, (TILES - 1) // 2) as i:
                    tile(i * 2 + 1, 1)
                    tile(i * 2 + 2, 0)

            @block.scalar
            def _(act):
                credit(act, [hi_ready, tanh_ready])
                act.wait_ge(gate_consts_landed, 48)
                act.activation(gate_mult[DECAY:DECAY + GH, :], gate_mult[DECAY:DECAY + GH, :], ACT.Exp)\
                   .then_inc(gate_mult_ready, 1)
                act.wait_ge(gate_y_abs, 1)
                act.activation(res[0][0:GATES, :], acc[0:GATES, :], ACT.Exp, scale=-1.0).then_inc(gate_exp, 1)
                act.wait_ge(gate_exp, 1)
                act.activation(res[0][0:GATES, :], res[0][0:GATES, :], ACT.Ln, bias=1.0).then_inc(gate_ln, 1)
                act.wait_ge(gate_cum, 1)
                act.activation(hi[FORGET:FORGET + FH, :], res[0][FORGET:FORGET + FH, :], ACT.Copy, scale=-1.0)\
                   .then_inc(neg_cum_ready, 1)
                act.activation(res[0][BETA:BETA + GH, :], acc[BETA:BETA + GH, :], ACT.Exp).then_inc(beta_ready, 1)

                act.wait_ge(pad_set, 1)
                act.wait_ge(gates_stored, 32)
                with act.Fori(0, 6) as i:
                    for j in range(2):
                        par = (CONV_AT + j) % 2
                        act.wait_ge(projected, i * 2 + (CONV_AT + j + 1))
                        act.wait_ge(conv_ready, i * 2 + after(j - 1))
                        act.activation(u[:, PAD:], banks[par][:], ACT.Copy).then_inc(u_ready, 1)
                        act.wait_ge(conv_ready, i * 2 + after(j))
                        act.wait_ge(stored[par], i * 16 + 16)
                        act.activation(res[par][:], acc[:], ACT.Tanh, scale=0.5).then_inc(tanh_ready, 1)
                with act.Fori(0, 4) as i:
                    for j in range(2):
                        par = (Z_AT + j) % 2
                        act.wait_ge(projected, i * 2 + (Z_AT + j + 1))
                        act.wait_ge(stored[par], i * 16 + (16 + 6 * 16))
                        act.activation(res[par][:], banks[par][:], ACT.Tanh, scale=0.5).then_inc(tanh_ready, 1)
                with act.Fori(0, 4) as i:
                    for j in range(2):
                        par = (QK_AT + j) % 2
                        act.wait_ge(projected, i * 2 + (QK_AT + j + 1))
                        act.wait_ge(lo_ready, i * 2 + after(j - 1))
                        act.wait_ge(qk_stored, i * 64 + (32 * j + 32))
                        act.activation(hi[:], banks[par][:], ACT.Copy, scale=(FD ** -0.5, 1.0)[j]).then_inc(hi_ready, 1)

            @block.vector
            def _(dve):
                credit(dve, [bank_read, conv_ready, result_ready, lo_ready])
                for k in range(KT):
                    dve.wait_ge(x_landed[k % 2], 16 * (k // 2 + 1))
                    dve.tensor_copy(x_hi[:, k, :], res[k % 2][:]).then_inc(x_hi_ready, 1)
                    dve.wait_ge(x_hi_ready, k + 1)
                    dve.tensor_tensor(x_lo[:, k, :], res[k % 2][:], x_hi[:, k, :].bitcast(F32),
                                      ALU.subtract).then_inc(x_split, 1)
                mask, y = res[1][0:GATES, :], u[0:GATES, PAD:]
                dve.wait_ge(x_split, KT)
                dve.memset(mask, 1.0).then_inc(scan_mask_set, 1)
                dve.wait_ge(scan_mask_set, 1)
                dve.memset(res[1][DECAY:DECAY + GH, :].rearrange("p (c t) -> p c t", t=CHUNK)[:, :, 0:1], 0.0)\
                   .then_inc(scan_mask_set, 1)
                dve.wait_ge(projected, 1)
                dve.wait_ge(gate_consts_set, 2)
                dve.wait_ge(gate_consts_landed, 48)
                dve.tensor_scalar(y, banks[0][0:GATES, :], gate_bias[:], gate_sign[:], ALU.add, ALU.mult)\
                   .then_inc(bank_read, 1)
                dve.wait_ge(bank_read, after(0))
                dve.scalar_tensor_tensor(acc[0:GATES, :], y, -1.0, y, ALU.mult, ALU.max).then_inc(gate_y_abs, 1)
                dve.wait_ge(gate_ln, 1)
                dve.scalar_tensor_tensor(acc[0:GATES, :], y, 0.0, res[0][0:GATES, :], ALU.min, ALU.subtract)\
                   .then_inc(gate_log, 1)
                dve.wait_ge(gate_log, 1)
                dve.wait_ge(gate_mult_ready, 1)
                dve.tensor_scalar(y, acc[0:GATES, :], gate_mult[:], None, ALU.mult).then_inc(gate_log_scaled, 1)
                dve.wait_ge(gate_log_scaled, 1)
                dve.wait_ge(scan_mask_set, 2)
                dve.tensor_tensor_scan(res[0][0:GATES, :], mask, y, 0.0, ALU.mult, ALU.add).then_inc(gate_cum, 1)

                dve.wait_ge(taps_landed, 16)
                dve.wait_ge(beta_ready, 1)
                with dve.Fori(0, 6) as i:
                    for j in range(2):
                        par = (CONV_AT + j) % 2
                        n = i * 2 + j
                        dve.wait_ge(conv_ready, i * 2 + after(j - 1))
                        dve.tensor_copy(tap[:], taps[:, n, :]).then_inc(conv_step, 1)
                        dve.wait_ge(u_ready, i * 2 + (j + 1))
                        dve.wait_ge(conv_step, i * 6 + (3 * j + 1))
                        dve.wait_ge(result_ready, i * 2 + after(j - 1))
                        dve.tensor_scalar(acc[:], u[:, PAD:], tap[:, 3:4], None, ALU.mult).then_inc(bank_read, 1)
                        dve.wait_ge(bank_read, i * 2 + after(CONV_AT + j))
                        for m in range(3):
                            dve.scalar_tensor_tensor(acc[:], u[:, PAD - 3 + m:PAD - 3 + m + SEQ], tap[:, m:m + 1],
                                                     acc[:], ALU.mult, ALU.add)\
                               .then_inc(conv_step if m < 2 else conv_ready, 1)
                            if m < 2:
                                dve.wait_ge(conv_step, i * 6 + (3 * j + 2 + m))
                        dve.wait_ge(conv_ready, i * 2 + after(j))
                        dve.wait_ge(tanh_ready, i * 2 + after(j))
                        dve.scalar_tensor_tensor(res[par][:], res[par][:], 1.0, acc[:], ALU.add, ALU.mult)\
                           .then_inc(result_ready, 1)
                with dve.Fori(0, 4) as i:
                    for j in range(2):
                        par = (Z_AT + j) % 2
                        dve.wait_ge(tanh_ready, i * 2 + after(12 + j))
                        dve.scalar_tensor_tensor(res[par][:], res[par][:], 1.0, banks[par][:], ALU.add, ALU.mult)\
                           .then_inc(result_ready, 1)
                        dve.wait_ge(result_ready, i * 2 + after(12 + j))
                        dve.sem_inc(bank_read, 1)
                with dve.Fori(0, 4) as i:
                    for j in range(2):
                        par = (QK_AT + j) % 2
                        dve.wait_ge(hi_ready, i * 2 + after(j))
                        dve.wait_ge(qk_stored, i * 64 + (32 * j + 32))
                        dve.scalar_tensor_tensor(lo[:], banks[par][:], (FD ** -0.5, 1.0)[j], hi[:].bitcast(F32),
                                                 ALU.mult, ALU.subtract).then_inc(lo_ready, 1)
                        dve.wait_ge(lo_ready, i * 2 + after(j))
                        dve.sem_inc(bank_read, 1)
                for j in range(4):
                    par = (V_AT + j) % 2
                    dve.wait_ge(projected, V_AT + j + 1)
                    dve.wait_ge(stored[par], 16 + 16 * (10 + j // 2))
                    dve.tensor_copy(res[par][:], banks[par][:]).then_inc(result_ready, 1)
                    dve.wait_ge(result_ready, after(20 + j))
                    dve.sem_inc(bank_read, 1)


BODIES = FH // 2
HEAD_UNITS = [(g, kb) for g in range(NB) for kb in range(4 * (g + 1))]
UNITS = 2 * len(HEAD_UNITS)
LAG = 2
SLOTS = UNITS + LAG
PLACES = 3
GROUPS = 2 * NB
CHUNKS = NCH // BODIES
LEVELS = 6
SH = GH // 2
(SQ, SS, TVK, TKN, GQ, TX, LEVEL) = range(7)
KS, VN, OD, SUMS, NORM, TY, ITEMS = range(LEVEL + 2 * LEVELS, LEVEL + 2 * LEVELS + 7)
STREAM_LAG = 3


def gdn_places():
    at = [[[] for _ in range(PLACES)] for _ in range(SLOTS)]
    ticks = 2 * (CHUNKS * ITEMS + STREAM_LAG)
    for t in range(CHUNKS * ITEMS):
        for a in range(2):
            slot, place = divmod((2 * (t + a * STREAM_LAG) + a) * PLACES * SLOTS // ticks, PLACES)
            at[slot][place].append((*divmod(t, ITEMS), a))
    return at


GDN_AT = gdn_places()


def slot_after(chunk):
    return 0 if chunk < 0 else next(s + 1 for s in range(SLOTS) for place in GDN_AT[s] if (chunk, TY, 1) in place)


def maxima_of(hp, g):
    return [("max", hp, g, a, kb4) for a in range(4) for kb4 in range(g + 1)]


def aux_items():
    at = [[[] for _ in range(PLACES)] for _ in range(SLOTS)]
    for b, s in enumerate((0, 2, 9, 13)):
        at[s][0].append(("v", b))

    def spread(hp, g, first, slots):
        items = maxima_of(hp, g)
        places = [(first + i, q) for i in range(slots) for q in range(PLACES)][:-1]
        for i, item in enumerate(items):
            s, q = places[i * len(places) // len(items)]
            at[s][q].append(item)
        at[first + slots][1].append(("row", hp, g))

    for hp in range(2):
        start = [hp * len(HEAD_UNITS) + HEAD_UNITS.index((g, 0)) for g in range(NB)]
        spread(hp, 2, start[0], 10)
        spread(hp, 3, start[2], 10)
        spread(hp + 1, 0, start[3], 5)
        spread(hp + 1, 1, start[3] + 6, 8)
        for g in range(NB):
            s = start[g] + 4 * g + 3 + LAG
            at[min(s + 1, SLOTS - 1)][0 if s + 1 < SLOTS else 2].append(("sum", hp, g))
            at[min(s + 2, SLOTS - 1)][2].append(("scale", hp, g))
    return at


AUX_AT = aux_items()
FIRST_AUX = maxima_of(0, 0) + [("row", 0, 0)] + maxima_of(0, 1) + [("row", 0, 1)]
AUX = [x for slot in AUX_AT for place in slot for x in place]
AUX_INDEX = {x: n for n, x in enumerate(FIRST_AUX + AUX)}


def unit(s):
    hp, u = divmod(s, len(HEAD_UNITS))
    g, kb = HEAD_UNITS[u]
    d = kb - 4 * g
    off = P * min(max(d, 0), 2)
    return hp, g, kb, off, d >= 0, slice(0 if d == 3 else P, 2 * P)


def halves(ap, b, odd):
    if len(ap.shape) == 3:
        return ap.rearrange("p h (g two b) -> p h g two b", two=2, b=b)[:, :, :, odd, :]
    return ap.rearrange("p (g two b) -> p g two b", two=2, b=b)[:, :, odd, :]


def blocks(ap, b):
    return ap.rearrange("p h (g b) -> p h g b", b=b) if len(ap.shape) == 3 else ap.rearrange("p (g b) -> p g b", b=b)


STEPS = [k for k in range(ITEMS) if k not in (SQ, SUMS, NORM)]


def step_at(n, k):
    return n * len(STEPS) + (STEPS.index(k) + 1)


def mix(nc, io, scr):
    with ExitStack() as ctx:
        def sb(name, shape, dt=F32):
            return ctx.enter_context(nc.sbuf_tensor("m_" + name, shape, dt))

        def bank(name):
            return ctx.enter_context(nc.psum_tensor("m_" + name, [P, 512], F32))

        def sem(name):
            return ctx.enter_context(nc.semaphore("m_" + name))

        ident = sb("ident", [P, P])
        ident_b = sb("ident_b", [P, P], BF16)
        masks = sb("masks", [P, LEVELS + 3, P])
        over_q = sb("over_q", [P, 2 * P], BF16)
        over_k = sb("over_k", [P, 2 * P], BF16)
        ones = sb("ones", [P, FD])
        ones_r = sb("ones_r", [P, 1], F32R)
        half = sb("half", [P, SH])
        norm_w = sb("norm_w", [P, 1])
        half_w = sb("half_w", [P, 1])
        fcol = sb("fcol", [P, FH, NCH])
        gcol = sb("gcol", [P, NCH, 3 * GH])
        K1 = [sb(f"K1_{i}", [P, SEQ], F32R) for i in range(2)]
        K2 = [sb(f"K2_{i}", [FD + 2, SEQ], F32R) for i in range(2)]
        Q1 = [sb(f"Q1_{i}", [P, 512], F32R) for i in range(4)]
        Q2 = [sb(f"Q2_{i}", [FD + 2, 512], F32R) for i in range(4)]
        QM = [sb(f"QM_{i}", [FD + 2, 512], F32R) for i in range(2)]
        zb = [sb(f"zb_{i}", [FD, 512]) for i in range(2)]
        v_feat = sb("v_feat", [P, SEQ])
        cols = v_feat[:, 0:NCH * GATES].rearrange("p (c r) -> p c r", r=GATES)
        v_hi = sb("v_hi", [P, NCH, 2, FD + 1], F32R)
        v_lo = sb("v_lo", [P, NCH, 2, FD], F32R)
        fbias = [sb(f"fbias{i}", [P, NCH]) for i in range(2)]
        p = [sb(f"p{i}", [P, 512]) for i in range(2)]
        p_hi = [sb(f"p_hi{i}", [P, 512], F32R) for i in range(3)]
        p_lo = [sb(f"p_lo{i}", [P, 512], F32R) for i in range(2)]
        maxima = sb("maxima", [P, 4, 4])
        mcol = sb("mcol", [P, 4], F32R)
        max_diag = sb("max_diag", [P, 4, P], F32R)
        den = sb("den", [1, 512])
        rcol = sb("rcol", [P, 4])
        rec_diag = sb("rec_diag", [P, 4, P])
        gated = sb("gated", [FD, 512])
        yb = [sb(f"yb{i}", [FD, 512]) for i in range(2)]
        H4 = [P, GH, P]
        cin = [sb(f"cin{i}", [P, 12, P]) for i in range(2)]
        grow = [sb(f"grow{i}", H4) for i in range(2)]
        brow = [sb(f"brow{i}", H4) for i in range(2)]
        za = [sb(f"za{i}", H4) for i in range(2)]
        ya = [sb(f"ya{i}", H4) for i in range(2)]
        cc = [sb(f"cc{i}", [P, 3 * GH]) for i in range(2)]
        sq = sb("sq", [P, 2 * GH, P])
        qe, kk, rk, so, ro = ([sb(f"{n}{a}", [P, SH]) for a in range(2)] for n in ("qe", "kk", "rk", "so", "ro"))
        (kn, vb, kT, kend, DT, DTb, eg, LT, intra, qg, X, XT, R2, vn, S, on) = (
            sb(n, H4) for n in ("kn", "vb", "kT", "kend", "DT", "DTb", "eg", "LT", "intra", "qg", "X", "XT", "R2",
                                "vn", "S", "on"))
        C = [sb(f"C{i}", H4) for i in range(LEVELS + 1)]
        T1 = [sb(f"T1_{i}", H4) for i in range(LEVELS)]
        aux = [bank(f"aux{i}") for i in range(2)]
        st = [bank(f"st{i}") for i in range(2)]
        pv = [bank(f"pv{i}") for i in range(2)]
        gd = [bank(f"gd{i}") for i in range(2)]
        gd4 = [b[:].rearrange("p (h t) -> p h t", t=P) for b in gd]
        gd8 = [b[:].rearrange("p (h t) -> p h t", t=P // 2) for b in gd]

        (consts_landed, gates_landed, cols_in_psum, cols_ready, gcol_ready, max_rows_set, ones_set, beta_exp_ready,
         consts_split, rows_set, half_w_ready, C_zeroed, T1_zeroed) = (sem(n) for n in (
             "consts_landed", "gates_landed", "cols_in_psum", "cols_ready", "gcol_ready", "max_rows_set", "ones_set",
             "beta_exp_ready", "consts_split", "rows_set", "half_w_ready", "C_zeroed", "T1_zeroed"))
        K_rows_set, ident_landed = sem("K_rows_set"), sem("ident_landed")
        K1_landed = [sem(f"K1_landed{i}") for i in range(2)]
        K2_landed = [sem(f"K2_landed{i}") for i in range(2)]
        Q_landed = [sem(f"Q_landed{i}") for i in range(4)]
        QM_landed = [sem(f"QM_landed{i}") for i in range(2)]
        zb_landed = [sem(f"zb_landed{i}") for i in range(2)]
        yb_stored = [sem(f"yb_stored{i}") for i in range(2)]
        (v_landed, heads_scored, fbias_ready, aux_ready, aux_used, v_hi_ready, mcol_ready, max_diag_ready, row_ready,
         scores_ready, p_ready, p_hi_ready, p_lo_ready, pv_done, den_ready, rcol_ready, rec_diag_ready, gated_ready,
         yb_ready) = (sem(n) for n in (
             "v_landed", "heads_scored", "fbias_ready", "aux_ready", "aux_used", "v_hi_ready", "mcol_ready",
             "max_diag_ready", "row_ready", "scores_ready", "p_ready", "p_hi_ready", "p_lo_ready", "pv_done",
             "den_ready", "rcol_ready", "rec_diag_ready", "gated_ready", "yb_ready"))
        g_landed = [sem(f"g_landed{i}") for i in range(2)]
        ya_stored = [sem(f"ya_stored{i}") for i in range(2)]
        g_step, C_ready, XT_ready, T1_ready = ([sem(f"{n}{a}") for a in range(2)] for n in (
            "g_step", "C_ready", "XT_ready", "T1_ready"))
        (cc_ready, dd0_ready, dd_ready, eg_ready, DT_ready, DTb_ready, sq_ready, kk_ready, rk_ready, kn_ready,
         kT_ready, qg_ready, kend_ready, LT_ready, intra_ready, XT0_off_ready, XT0_ready, X0_ready, R2_ready,
         vn_ready, sqo_ready,
         so_ready, mo_ready, ro_ready, on_ready, S_ready, ya_ready) = (sem(n) for n in (
             "cc_ready", "dd0_ready", "dd_ready", "eg_ready", "DT_ready", "DTb_ready", "sq_ready", "kk_ready",
             "rk_ready", "kn_ready", "kT_ready", "qg_ready", "kend_ready", "LT_ready", "intra_ready", "XT0_off_ready",
             "XT0_ready",
             "X0_ready", "R2_ready", "vn_ready", "sqo_ready", "so_ready", "mo_ready", "ro_ready", "on_ready",
             "S_ready", "ya_ready"))

        chunked = {
            "conv": scr["feat"][CONV_T:CONV_T + 12].rearrange("t p (c s) -> c p t s", s=P),
            "za": scr["feat"][ZA_T:ZA_T + GH].rearrange("t p (c s) -> c p t s", s=P),
            "ya": scr["mixT"][0:GH].rearrange("t p (c s) -> c p t s", s=P),
            "gates": scr["gates"].rearrange("r (c s) -> c r s", s=P),
        }
        paired = {n: scr[n].rearrange("i (h d) s -> i h d s", h=2) for n in ("q_hi", "q_lo", "k_hi", "k_lo")}
        paired["zb"] = scr["feat"][ZB_T:ZB_T + 4].rearrange("i (h d) s -> i h d s", h=2)
        paired["yb"] = scr["mixT"][GH:2 * GH].rearrange("i (h d) s -> i h d s", h=2)
        cum_rows = scr["neg_cum"].rearrange("(i h) s -> i h s", h=2)

        with nc.Block() as block:
            @block.sync
            def _(sp):
                for i in range(2):
                    sp.sem_inc(yb_stored[i], 16)
                    sp.sem_inc(ya_stored[i], 16)

                def load_keys(i, hp):
                    sp.dma_start(K2[hp][0:FD, :].bitcast(F32), paired["k_hi"][i][hp]).then_inc(K2_landed[hp], 16)
                    sp.dma_start(K2[hp][FD + 1:FD + 2, :].bitcast(F32), cum_rows[i][hp:hp + 1]).then_inc(K2_landed[hp], 16)
                    sp.dma_start(K1[hp][0:FD, :].bitcast(F32), paired["k_hi"][i][hp]).then_inc(K1_landed[hp], 16)
                    sp.dma_start(K1[hp][FD:P, :].bitcast(F32), paired["k_lo"][i][hp]).then_inc(K1_landed[hp], 16)

                def load_max_queries(i, G):
                    hp, g = G // NB % 2, G % NB
                    sp.dma_start(QM[G % 2][0:FD, :].bitcast(F32), paired["q_hi"][i][hp][:, g * 512:(g + 1) * 512])\
                      .then_inc(QM_landed[G % 2], 16)

                def load_queries(i, G):
                    hp, g = G // NB % 2, G % NB
                    b = G % 4
                    cut = slice(g * 512, (g + 1) * 512)
                    for dst, src in ((Q1[b][0:FD, :], "q_hi"), (Q1[b][FD:P, :], "q_hi"), (Q2[b][0:FD, :], "q_lo")):
                        sp.dma_start(dst.bitcast(F32), paired[src][i][hp][:, cut]).then_inc(Q_landed[b], 16)

                def load_z(i, G):
                    hp, g = G // NB % 2, G % NB
                    sp.dma_start(zb[G % 2][:], paired["zb"][i][hp][:, g * 512:(g + 1) * 512]).then_inc(zb_landed[G % 2], 16)

                def load_chunk(n, par):
                    for tile, row in ((grow, DECAY), (brow, BETA)):
                        rows = chunked["gates"][n][row:row + GH].unsqueeze(0).broadcast_to(H4)
                        sp.dma_start(tile[par][:], rows).then_inc(g_landed[par], 16)
                    sp.dma_start(cin[par][:], chunked["conv"][n]).then_inc(g_landed[par], 16)
                    sp.dma_start(za[par][:], chunked["za"][n]).then_inc(g_landed[par], 16)

                gates = flat(cin[0][:])
                sp.dma_start(gates[0:GATES, :], scr["gates"][:, 0:12 * P]).then_inc(gates_landed, 16)
                sp.dma_start(flat(cin[1][:])[0:GATES, 0:SEQ - 12 * P], scr["gates"][:, 12 * P:]).then_inc(gates_landed, 16)
                sp.dma_start(ident[:], io["ident"]).then_inc(ident_landed, 16)
                sp.wait_ge(K_rows_set, 2)
                sp.wait_ge(rows_set, 2)
                load_max_queries(0, 0)
                sp.dma_start(masks[:], io["masks"]).then_inc(consts_landed, 16)
                sp.dma_start(norm_w[:], io["norm_w"]).then_inc(consts_landed, 16)
                load_keys(0, 0)
                load_queries(0, 0)
                sp.wait_ge(cols_in_psum, 4)
                load_chunk(0, 0)
                load_max_queries(0, 1)
                load_queries(0, 1)
                sp.wait_ge(gcol_ready, 2)
                sp.dma_start(v_feat[:], scr["feat"][VB_T]).then_inc(v_landed, 16)
                load_z(0, 0)
                load_z(0, 1)

                with sp.Fori(0, BODIES) as it:
                    after_it = (it + 1) % BODIES
                    for s in range(SLOTS + 1):
                        for G in range(2, GROUPS + 2):
                            if s == (G - 2) // NB * len(HEAD_UNITS) + HEAD_UNITS.index(((G - 2) % NB, 0)):
                                i = it if G < GROUPS else after_it
                                sp.wait_ge(mcol_ready, it * GROUPS + after(G - 2))
                                load_max_queries(i, G)
                                sp.wait_ge(yb_ready, it * GROUPS + after(G - 4))
                                load_queries(i, G)
                        if s == 0:
                            sp.wait_ge(heads_scored, it * 2 + after(-1))
                            load_keys(it, 1)
                        if s == UNITS // 2 + 1:
                            sp.wait_ge(heads_scored, it * 2 + after(0))
                            load_keys(after_it, 0)
                            sp.wait_ge(aux_used, it * len(AUX) + after(AUX_INDEX["v", 3]))
                            sp.dma_start(v_feat[:], scr["feat"][VB_T:VB_T + 4][after_it]).then_inc(v_landed, 16)
                        for j in range(CHUNKS + 1):
                            if s == slot_after(j - 1):
                                sp.wait_ge(ya_ready, it * (2 * CHUNKS) + after(2 * (j - 1) + 1))
                                if j > 0:
                                    sp.dma_start(chunked["ya"][it * CHUNKS + (j - 1)], ya[(j - 1) % 2][:])\
                                      .then_inc(ya_stored[(j - 1) % 2], 16)
                                if j < CHUNKS:
                                    load_chunk((it * CHUNKS + (j + 1)) % NCH, (j + 1) % 2)
                        for kind, *what in AUX_AT[s][2] if s < SLOTS else ():
                            if kind == "scale":
                                hp, g = what
                                G = hp * NB + g
                                sp.wait_ge(yb_ready, it * GROUPS + after(G))
                                sp.dma_start(paired["yb"][it][hp][:, g * 512:(g + 1) * 512], yb[G % 2][:])\
                                  .then_inc(yb_stored[G % 2], 16)
                                load_z(it if G + 2 < GROUPS else after_it, G + 2)
                for i in range(2):
                    sp.wait_ge(ya_stored[i], 16 + 16 * NCH // 2)
                    sp.wait_ge(yb_stored[i], 16 + 16 * BODIES * GROUPS // 2)
                    sp.wait_ge(K1_landed[i], 32 * (BODIES + 1 - i))
                    sp.wait_ge(K2_landed[i], 32 * (BODIES + 1 - i))
                    sp.wait_ge(g_landed[i], 64 * (NCH // 2 + 1 - i))
                    sp.wait_ge(QM_landed[i], 16 * (BODIES * GROUPS // 2 + 1))
                    sp.wait_ge(zb_landed[i], 16 * (BODIES * GROUPS // 2 + 1))
                    sp.wait_ge(Q_landed[i], 48 * (BODIES * GROUPS // 4 + 1))
                sp.wait_ge(v_landed, 16 * (BODIES + 1))

            @block.tensor
            def _(pe):
                credit(pe, [aux_ready, heads_scored, scores_ready, pv_done])
                pe.wait_ge(gates_landed, 32)
                pe.wait_ge(ident_landed, 16)
                for q, b in enumerate((aux[0], aux[1], st[0], st[1])):
                    for i in range(4):
                        c = 4 * q + i
                        src = flat(cin[c // 12][:])[0:GATES, c % 12 * P:(c % 12 + 1) * P]
                        mm = pe.transpose(b[:, i * P:i * P + GATES], src, ident[0:GATES, 0:GATES])
                    mm.then_inc(cols_in_psum, 1)
                pe.wait_ge(cols_ready, 4)
                pe.wait_ge(consts_split, 5)
                pe.wait_ge(rows_set, 2)
                pe.wait_ge(ones_set, 1)

                def do_aux(item, it=0):
                    kind, *what = item
                    m = AUX_INDEX[item]
                    b = aux[m % 2]
                    pe.wait_ge(aux_used, it * len(AUX) + after(m - 2))
                    if kind == "v":
                        if what[0] == 0:
                            pe.wait_ge(v_landed, it * 16 + 16)
                        for i in range(4):
                            c = what[0] * 4 + i
                            mm = pe.transpose(b[:, i * P:(i + 1) * P], v_feat[:, c * P:(c + 1) * P], ident[:])
                    elif kind == "max":
                        hp, g, a, kb4 = what
                        G = hp * NB + g
                        if a == 0 and kb4 == 0:
                            pe.wait_ge(QM_landed[G % 2], it * 64 + (16 * (G // 2) + 16))
                            pe.wait_ge(K2_landed[hp % 2], it * 32 + (32 * (hp // 2) + 32))
                        diagonal = kb4 == g
                        n = max(a + 1, 2) * P if diagonal else 512
                        mm = pe.matmul(b[:, 0:n], QM[G % 2][:, a * P:(a + 1) * P],
                                       K2[hp % 2][:, kb4 * 512:kb4 * 512 + n], start=True, stop=not diagonal)
                        if diagonal:
                            mm = pe.matmul(b[:, a * P:n], ident_b[:], over_q[:, 0:n - a * P], start=False, stop=True)
                    elif kind == "row":
                        hp, g = what
                        pe.wait_ge(max_diag_ready, it * GROUPS + after(hp * NB + g))
                        mm = pe.matmul(b[0:1, :], ones_r[:], flat(max_diag[:]), start=True, stop=True)
                    elif kind == "sum":
                        hp, g = what
                        pe.wait_ge(den_ready, it * GROUPS + after(hp * NB + g))
                        for a in range(4):
                            mm = pe.matmul(b[:, a:a + 1], den[:, a * P:(a + 1) * P], ones[0:1, 0:1], start=True, stop=True)
                    else:
                        hp, g = what
                        pe.wait_ge(rec_diag_ready, it * GROUPS + after(hp * NB + g))
                        mm = pe.matmul(b[0:FD, :], ones[:], flat(rec_diag[:]), start=True, stop=True)
                    mm.then_inc(aux_ready, 1)

                for item in FIRST_AUX:
                    do_aux(item)
                with pe.Fori(0, BODIES) as it:
                    def scores(s):
                        hp, g, kb, off, diagonal, cut = unit(s)
                        G = hp * NB + g
                        b = st[s % 2]
                        if kb == 0:
                            pe.wait_ge(K1_landed[hp], it * 32 + 32)
                            pe.wait_ge(Q_landed[G % 4], it * 96 + (48 * (G // 4) + 48))
                            pe.wait_ge(row_ready, it * GROUPS + after(G))
                        pe.wait_ge(p_hi_ready, it * UNITS + after(s - 2))
                        keys = slice(kb * P, (kb + 1) * P)
                        pe.matmul(b[:, off:], K1[hp][:, keys], Q1[G % 4][:, off:], start=True, stop=False)
                        mm = pe.matmul(b[:, off:], K2[hp][:, keys], Q2[G % 4][:, off:], start=False, stop=not diagonal)
                        if diagonal:
                            mm = pe.matmul(b[:, off:off + cut.stop - cut.start], ident_b[:], over_k[:, cut],
                                           start=False, stop=True)
                        mm.then_inc(scores_ready, 1)
                        if s % len(HEAD_UNITS) == len(HEAD_UNITS) - 1:
                            pe.wait_ge(scores_ready, it * UNITS + after(s))
                            pe.sem_inc(heads_scored, 1)

                    def values(s):
                        hp, g, kb, off, diagonal, _ = unit(s)
                        G = hp * NB + g
                        b = pv[G % 2]
                        if kb == 0:
                            pe.wait_ge(gated_ready, it * GROUPS + after(G - 2))
                        pe.wait_ge(p_hi_ready, it * UNITS + after(s))
                        last = kb == 4 * g + 3
                        pe.matmul(b[0:FD + 1, off:], v_hi[:, kb, hp, :], p_hi[s % 3][:, off:], start=kb == 0, stop=False)
                        pe.matmul(b[0:FD, off:], v_lo[:, kb, hp, :], p_hi[s % 3][:, off:], start=False, stop=False)
                        pe.wait_ge(p_lo_ready, it * UNITS + after(s))
                        pe.matmul(b[0:FD + 1, off:], v_hi[:, kb, hp, :], p_lo[s % 2][:, off:], start=False, stop=last)\
                          .then_inc(pv_done, 1)

                    def gdn(j, k, a):
                        n = it * CHUNKS + j
                        m = n * 2 + a
                        par = j % 2
                        b, b64 = gd4[a], gd8[a]
                        heads = range(a * SH, (a + 1) * SH)

                        def product(lhsT, rhs):
                            for i, h in enumerate(heads):
                                mm = pe.matmul(b[:, i, :], lhsT[:, h, :], rhs[:, h, :], start=True, stop=True)
                            return mm

                        def turned(tile):
                            for i, h in enumerate(heads):
                                mm = pe.transpose(b[:, i, :], tile[:, h, :], ident[:])
                            return mm

                        if k == SS:
                            pe.wait_ge(sq_ready, m + after(0))
                            pe.wait_ge(ya_ready, m + after(-2))
                            for i, h in enumerate(heads):
                                pe.matmul(gd[a][:, i:i + 1], sq[:, h, :], ones[:, 0:1], start=True, stop=True)
                                mm = pe.matmul(gd[a][:, SH + i:SH + i + 1], sq[:, GH + h, :], ones[:, 0:1], start=True, stop=True)
                        elif k == TVK:
                            pe.wait_ge(g_landed[par], it * 128 + (64 * (j // 2) + 64))
                            pe.wait_ge(kk_ready, m + after(0))
                            for i, h in enumerate(heads):
                                pe.transpose(b[:, i, :], cin[par][:, 2 * GH + h, :], ident[:])
                                mm = pe.transpose(b[:, SH + i, :], cin[par][:, GH + h, :], ident[:])
                        elif k == TKN:
                            pe.wait_ge(kn_ready, m + after(0))
                            mm = turned(kn)
                        elif k == GQ:
                            pe.wait_ge(kT_ready, m + after(0))
                            for i, h in enumerate(heads):
                                pe.matmul(b[:, i, :], kT[:, h, :], kT[:, h, :], start=True, stop=True)
                                mm = pe.matmul(b[:, SH + i, :], kT[:, h, :], cin[par][:, h, :], start=True, stop=True)
                        elif k == TX:
                            pe.wait_ge(intra_ready, m + after(0))
                            pe.wait_ge(XT0_ready, m + after(0))
                            mm = turned(XT)
                        elif LEVEL <= k < KS:
                            lv, part = divmod(k - LEVEL, 2)
                            width = 2 << lv
                            if part == 0:
                                pe.wait_ge(C_ready[a], n * (LEVELS + 1) + after(lv + 1))
                                if lv == 0:
                                    pe.wait_ge(X0_ready, m + after(0))
                                else:
                                    pe.wait_ge(XT_ready[a], n * LEVELS + after(lv - 1))
                                for i, h in enumerate(heads):
                                    mm = pe.matmul(blocks(b64[:, i, :], width), C[lv + 1][:, h, :],
                                                   halves(X[:, h, :], width, 0), start=True, stop=True)
                            else:
                                pe.wait_ge(T1_ready[a], n * LEVELS + after(lv))
                                for i, h in enumerate(heads):
                                    if lv < LEVELS - 1:
                                        pe.matmul(blocks(b64[:, i, :], width), XT[:, h, :],
                                                  halves(T1[lv][:, h, :], width, 0), start=True, stop=True)
                                    mm = pe.matmul(blocks(b64[:, SH + i, :], width), T1[lv][:, h, :],
                                                   halves(XT[:, h, :], width, 1), start=True, stop=True)
                        elif k == KS:
                            pe.wait_ge(S_ready, m + after(-2))
                            pe.wait_ge(XT_ready[a], n * LEVELS + after(LEVELS - 1))
                            mm = product(kT, S)
                        elif k == VN:
                            pe.wait_ge(R2_ready, m + after(0))
                            mm = product(XT, R2)
                        elif k == OD:
                            pe.wait_ge(qg_ready, m + after(0))
                            pe.wait_ge(kend_ready, m + after(0))
                            pe.wait_ge(vn_ready, m + after(0))
                            for i, h in enumerate(heads):
                                pe.matmul(b[:, i, :], qg[:, h, :], S[:, h, :], start=True, stop=False)
                                pe.matmul(b[:, i, :], intra[:, h, :], vn[:, h, :], start=False, stop=True)
                            for i, h in enumerate(heads):
                                mm = pe.matmul(b[:, SH + i, :], kend[:, h, :], vn[:, h, :], start=True, stop=True)
                        elif k == TY:
                            pe.wait_ge(S_ready, m + after(0))
                            pe.wait_ge(on_ready, m + after(0))
                            mm = turned(on)
                        if k in STEPS:
                            mm.then_inc(g_step[a], 1)

                    def place(s, q):
                        for item in AUX_AT[s][q]:
                            do_aux(item, it)
                        for j, k, a in GDN_AT[s][q]:
                            gdn(j, k, a)

                    for s in range(SLOTS):
                        if s < UNITS:
                            scores(s)
                        place(s, 0)
                        if s >= LAG:
                            values(s - LAG)
                        place(s, 1)
                        place(s, 2)

            @block.scalar
            def _(act):
                credit(act, [p_ready, p_hi_ready, eg_ready, DT_ready, sq_ready, kT_ready, X0_ready, *T1_ready,
                             vn_ready, sqo_ready])
                act.wait_ge(cols_ready, 4)
                act.activation(gcol[:, :, GH:2 * GH], cols[:, :, DECAY:DECAY + GH], ACT.Exp).then_inc(beta_exp_ready, 1)
                act.wait_ge(gcol_ready, 2)
                act.wait_ge(T1_zeroed, 1)
                with act.Fori(0, BODIES) as it:
                    def exp(s):
                        hp, g, kb, off, _, _ = unit(s)
                        if s % len(HEAD_UNITS) == 0:
                            act.wait_ge(fbias_ready, it * 2 + (hp + 1))
                        act.wait_ge(p_lo_ready, it * UNITS + after(s - 2))
                        act.wait_ge(scores_ready, it * UNITS + after(s))
                        act.activation(p[s % 2][:, off:], st[s % 2][:, off:], ACT.Exp, bias=fbias[hp][:, kb:kb + 1])\
                           .then_inc(p_ready, 1)
                        act.wait_ge(pv_done, it * UNITS + after(max(s - 3, -1)))
                        act.activation(p_hi[s % 3][:, off:], st[s % 2][:, off:], ACT.Exp, bias=fbias[hp][:, kb:kb + 1])\
                           .then_inc(p_hi_ready, 1)

                    def gdn(j, k, a):
                        n = it * CHUNKS + j
                        m = n * 2 + a
                        par = j % 2
                        mine = slice(a * SH, (a + 1) * SH)

                        def take(out, src, ready, func=ACT.Copy):
                            act.wait_ge(g_step[a], step_at(n, k))
                            act.activation(out, src, func).then_inc(ready, 1)

                        if k == SQ:
                            act.wait_ge(g_landed[par], it * 128 + (64 * (j // 2) + 64))
                            act.wait_ge(on_ready, m + after(-2))
                            act.activation(sq[:].rearrange("p (w h) t -> p w h t", w=2)[:, :, mine, :],
                                           cin[par][:, 0:2 * GH, :].rearrange("p (w h) t -> p w h t", w=2)[:, :, mine, :],
                                           ACT.Square).then_inc(sq_ready, 1)
                        elif k == SS:
                            act.wait_ge(S_ready, m + after(-2))
                            act.activation(eg[:, mine, :], grow[par][:, mine, :], ACT.Exp).then_inc(eg_ready, 1)
                            act.wait_ge(dd_ready, m + after(0))
                            act.activation(DT[:, mine, :], DT[:, mine, :], ACT.Exp).then_inc(DT_ready, 1)
                        elif k == TKN:
                            take(kT[:, mine, :], gd4[a][:, 0:SH, :], kT_ready)
                        elif k == TX:
                            take(X[:, mine, :], gd4[a][:, 0:SH, :], X0_ready)
                        elif LEVEL <= k < KS and (k - LEVEL) % 2 == 0:
                            lv = (k - LEVEL) // 2
                            take(halves(T1[lv][:, mine, :], 2 << lv, 0), blocks(gd8[a][:, 0:SH, :], 2 << lv), T1_ready[a])
                        elif k == VN:
                            take(vn[:, mine, :], gd4[a][:, 0:SH, :], vn_ready)
                        elif k == OD:
                            act.wait_ge(S_ready, m + after(0))
                            take(sq[:, mine, :], gd4[a][:, 0:SH, :], sqo_ready, ACT.Square)

                    for s in range(SLOTS):
                        for q in range(PLACES):
                            if q == 1 and s < UNITS:
                                exp(s)
                            for j, k, a in GDN_AT[s][q]:
                                gdn(j, k, a)

            @block.gpsimd
            def _(pool):
                credit(pool, [p_lo_ready, dd0_ready, dd_ready, DTb_ready, rk_ready, qg_ready, kend_ready, ro_ready,
                              *C_ready, max_diag_ready, rec_diag_ready])
                for i in range(4):
                    pool.memset(Q2[i][FD:FD + 2, :].bitcast(F32), 0.0)
                for i in range(2):
                    pool.memset(QM[i][FD:FD + 2, :].bitcast(F32), 1.0).then_inc(max_rows_set, 1)
                pool.wait_ge(max_rows_set, 2)
                for i in range(2):
                    pool.memset(QM[i][FD:FD + 1, :].bitcast(F32), 0.0).then_inc(rows_set, 1)
                pool.wait_ge(rows_set, 2)
                pool.memset(v_hi[:, :, :, FD:].bitcast(F32), 1.0)
                pool.memset(ones[:], 1.0)
                pool.memset(ones_r[:].bitcast(F32), 1.0)
                pool.memset(half[:], -0.5)
                pool.memset(S[:], 0.0).then_inc(ones_set, 1)
                pool.wait_ge(ones_set, 1)
                for tile in C:
                    zeroed = pool.memset(tile[:], 0.0)
                zeroed.then_inc(C_zeroed, 1)
                pool.wait_ge(ident_landed, 16)
                pool.wait_ge(consts_landed, 32)
                ident4 = ident[:].unsqueeze(1).broadcast_to([P, 4, P])

                def do_aux(item, it=0):
                    kind, *what = item
                    m = AUX_INDEX[item]
                    if kind == "max" and what[2] == 3 and what[3] == what[1]:
                        G = what[0] * NB + what[1]
                        pool.wait_ge(row_ready, it * GROUPS + after(G - 1))
                        pool.wait_ge(mcol_ready, it * GROUPS + after(G))
                        pool.tensor_tensor(max_diag[:], ident4, wide(mcol[:].bitcast(F32), P), ALU.mult)\
                            .then_inc(max_diag_ready, 1)
                    elif kind == "sum":
                        G = what[0] * NB + what[1]
                        pool.wait_ge(yb_ready, it * GROUPS + after(G - 1))
                        pool.wait_ge(rcol_ready, it * GROUPS + after(G))
                        pool.tensor_tensor(rec_diag[:], ident4, wide(rcol[:], P), ALU.mult).then_inc(rec_diag_ready, 1)

                for item in FIRST_AUX:
                    do_aux(item)
                pool.wait_ge(C_zeroed, 1)
                with pool.Fori(0, BODIES) as it:
                    def low(s):
                        off = unit(s)[3]
                        pool.wait_ge(pv_done, it * UNITS + after(s - 2))
                        pool.wait_ge(p_hi_ready, it * UNITS + after(s))
                        pool.tensor_tensor(p_lo[s % 2][:, off:], p[s % 2][:, off:], p_hi[s % 3][:, off:].bitcast(F32),
                                           ALU.subtract).then_inc(p_lo_ready, 1)

                    def gdn(j, k, a):
                        n = it * CHUNKS + j
                        m = n * 2 + a
                        par = j % 2
                        mine = slice(a * SH, (a + 1) * SH)
                        H2 = [P, SH, P]

                        def level(src, i):
                            b = 1 << i
                            mask = halves(masks[:, i, :], b, 1).unsqueeze(1).broadcast_to([P, SH, P // (2 * b), b])
                            pool.tensor_tensor(halves(C[i][:, mine, :], b, 1), halves(src[:, mine, :], b, 1), mask, ALU.mult)\
                                .then_inc(C_ready[a], 1)

                        if k == SQ:
                            pool.wait_ge(g_landed[par], it * 128 + (64 * (j // 2) + 64))
                            pool.wait_ge(cc_ready, n + after(0))
                            pool.wait_ge(LT_ready, m + after(-2))
                            pool.wait_ge(intra_ready, m + after(-2))
                            pool.tensor_tensor(DT[:, mine, :], grow[par][:, mine, :],
                                               wide(cc[par][:, 2 * GH + a * SH:2 * GH + (a + 1) * SH], P), ALU.subtract)\
                                .then_inc(dd0_ready, 1)
                            pool.wait_ge(dd0_ready, m + after(0))
                            pool.tensor_tensor(DT[:, mine, :], DT[:, mine, :], masks[:, LEVELS + 2:, :].broadcast_to(H2),
                                               ALU.add).then_inc(dd_ready, 1)
                        elif k == SS:
                            pool.wait_ge(kk_ready, m + after(0))
                            pool.tensor_tensor(rk[a][:], kk[a][:], half[:], ALU.pow).then_inc(rk_ready, 1)
                        elif k == TVK:
                            pool.wait_ge(DT_ready, m + after(0))
                            pool.tensor_tensor(DTb[:, mine, :], DT[:, mine, :], brow[par][:, mine, :], ALU.mult)\
                                .then_inc(DTb_ready, 1)
                            pool.wait_ge(DTb_ready, m + after(0))
                            level(DTb, 0)
                            pool.wait_ge(eg_ready, m + after(0))
                            pool.tensor_tensor(qg[:, mine, :], cin[par][:, mine, :], eg[:, mine, :], ALU.mult)\
                                .then_inc(qg_ready, 1)
                        elif k == TKN:
                            pool.wait_ge(kn_ready, m + after(0))
                            pool.tensor_tensor(kend[:, mine, :], kn[:, mine, :], DT[:, mine, P - 1:].broadcast_to(H2),
                                               ALU.mult).then_inc(kend_ready, 1)
                        elif k == GQ:
                            pool.wait_ge(LT_ready, m + after(0))
                            level(LT, 1)
                        elif TX <= k < TX + LEVELS - 1:
                            level(LT, k - TX + 2)
                        elif k == SUMS:
                            pool.wait_ge(mo_ready, m + after(0))
                            pool.tensor_tensor(ro[a][:], so[a][:], half[:], ALU.pow).then_inc(ro_ready, 1)

                    for s in range(SLOTS):
                        if 1 <= s <= UNITS:
                            low(s - 1)
                        for q in range(PLACES):
                            for item in AUX_AT[s][q]:
                                do_aux(item, it)
                            for j, k, a in GDN_AT[s][q]:
                                gdn(j, k, a)

            @block.vector
            def _(dve):
                credit(dve, [aux_used, mcol_ready, row_ready, den_ready, rcol_ready, gated_ready, yb_ready,
                             v_hi_ready, cc_ready, kk_ready, kn_ready, LT_ready, intra_ready, XT0_off_ready,
                             XT0_ready, *XT_ready, R2_ready, so_ready, mo_ready, on_ready, S_ready, ya_ready])
                for i in range(2):
                    dve.memset(K2[i][FD:FD + 2, :].bitcast(F32), 1.0).then_inc(K_rows_set, 1)
                dve.memset(over_q[:, P:], NEG)
                dve.memset(over_k[:, 0:P], NEG).then_inc(consts_split, 2)
                dve.wait_ge(ident_landed, 16)
                dve.wait_ge(consts_landed, 32)
                dve.tensor_copy(ident_b[:], ident[:]).then_inc(consts_split, 1)
                dve.tensor_copy(over_q[:, 0:P], masks[:, LEVELS + 1, :]).then_inc(consts_split, 1)
                dve.tensor_copy(over_k[:, P:], masks[:, LEVELS + 2, :]).then_inc(consts_split, 1)
                dve.tensor_scalar(half_w[:], norm_w[:], 0.5, None, ALU.mult).then_inc(half_w_ready, 1)
                for q, b in enumerate((aux[0], aux[1], st[0], st[1])):
                    dve.wait_ge(cols_in_psum, q + 1)
                    dve.tensor_copy(cols[:, 4 * q:4 * q + 4, :], b[:].rearrange("p (c r) -> p c r", c=4)[:, :, 0:GATES])\
                       .then_inc(cols_ready, 1)
                dve.wait_ge(cols_ready, 4)
                dve.tensor_scalar(gcol[:, :, 0:GH], cols[:, :, BETA:BETA + GH], 0.5, None, ALU.mult)
                dve.tensor_copy(gcol[:, :, 2 * GH:], cols[:, :, DECAY:DECAY + GH])
                dve.tensor_scalar(fcol[:].rearrange("p h c -> p c h"), cols[:, :, FORGET:FORGET + FH], -1.0, None, ALU.mult)\
                   .then_inc(gcol_ready, 1)
                dve.wait_ge(beta_exp_ready, 1)
                dve.scalar_tensor_tensor(gcol[:, :, GH:2 * GH], gcol[:, :, GH:2 * GH], -1.0, cols[:, :, BETA:BETA + GH],
                                         ALU.mult, ALU.mult).then_inc(gcol_ready, 1)
                dve.wait_ge(gcol_ready, 2)
                dve.wait_ge(half_w_ready, 1)
                dve.wait_ge(rows_set, 2)

                def do_aux(item, it=0):
                    kind, *what = item
                    m = AUX_INDEX[item]
                    b = aux[m % 2]

                    def came():
                        dve.wait_ge(aux_ready, it * len(AUX) + after(m))

                    if kind == "v":
                        cut = slice(what[0] * 4, what[0] * 4 + 4)
                        src = b[:].rearrange("p (c h d) -> p c h d", c=4, h=2)
                        if what[0] == 0:
                            dve.wait_ge(pv_done, it * UNITS + after(-1))
                        came()
                        dve.tensor_copy(v_hi[:, cut, :, 0:FD], src).then_inc(v_hi_ready, 1)
                        dve.wait_ge(v_hi_ready, it * 4 + after(what[0]))
                        dve.tensor_tensor(v_lo[:, cut, :, :], src, v_hi[:, cut, :, 0:FD].bitcast(F32), ALU.subtract)\
                           .then_inc(aux_used, 1)
                    elif kind == "max":
                        hp, g, a, kb4 = what
                        G = hp * NB + g
                        n = max(a + 1, 2) * P if kb4 == g else 512
                        if a == 0 and kb4 == 0:
                            dve.wait_ge(mcol_ready, it * GROUPS + after(G - 1))
                        came()
                        dve.reduce_max(maxima[:, a, kb4:kb4 + 1], b[:, 0:n], AX.X).then_inc(aux_used, 1)
                        if a == 3 and kb4 == g:
                            dve.wait_ge(aux_used, it * len(AUX) + after(m))
                            dve.wait_ge(max_diag_ready, it * GROUPS + after(G - 1))
                            dve.reduce_max(mcol[:], maxima[:, :, 0:g + 1], AX.X).then_inc(mcol_ready, 1)
                    elif kind == "row":
                        hp, g = what
                        G = hp * NB + g
                        dve.wait_ge(yb_ready, it * GROUPS + after(G - 4))
                        came()
                        dve.tensor_scalar(Q2[G % 4][FD:FD + 1, :], b[0:1, :], -1.0, None, ALU.mult).then_inc(row_ready, 1)
                        dve.wait_ge(row_ready, it * GROUPS + after(G))
                        dve.sem_inc(aux_used, 1)
                    elif kind == "sum":
                        hp, g = what
                        G = hp * NB + g
                        dve.wait_ge(rec_diag_ready, it * GROUPS + after(G - 1))
                        came()
                        dve.reciprocal(rcol[:], b[:, 0:4]).then_inc(rcol_ready, 1)
                        dve.wait_ge(rcol_ready, it * GROUPS + after(G))
                        dve.sem_inc(aux_used, 1)
                    else:
                        hp, g = what
                        G = hp * NB + g
                        dve.wait_ge(yb_stored[G % 2], it * (16 * GROUPS // 2) + (16 + 16 * (G // 2)))
                        came()
                        dve.scalar_tensor_tensor(yb[G % 2][:], gated[:], 0.5, b[0:FD, :], ALU.mult, ALU.mult)\
                           .then_inc(yb_ready, 1)
                        dve.wait_ge(yb_ready, it * GROUPS + after(G))
                        dve.sem_inc(aux_used, 1)

                for item in FIRST_AUX:
                    do_aux(item)
                for tile in T1:
                    zeroed = dve.memset(tile[:], 0.0)
                zeroed.then_inc(T1_zeroed, 1)
                with dve.Fori(0, BODIES) as it:
                    def finish(hp, g):
                        G = hp * NB + g
                        dve.wait_ge(pv_done, it * UNITS + after(hp * len(HEAD_UNITS) + HEAD_UNITS.index((g, 4 * g + 3))))
                        dve.tensor_copy(den[:], pv[G % 2][FD:FD + 1, :]).then_inc(den_ready, 1)
                        dve.wait_ge(zb_landed[G % 2], it * 64 + (16 * (G // 2) + 16))
                        dve.wait_ge(yb_ready, it * GROUPS + after(G - 1))
                        dve.wait_ge(den_ready, it * GROUPS + after(G))
                        dve.tensor_tensor(gated[:], pv[G % 2][0:FD, :], zb[G % 2][:], ALU.mult).then_inc(gated_ready, 1)

                    def gdn(j, k, a):
                        n = it * CHUNKS + j
                        m = n * 2 + a
                        par = j % 2
                        mine = slice(a * SH, (a + 1) * SH)
                        b = gd4[a][:, 0:SH, :]
                        b2 = gd4[a][:, SH:, :]

                        def came():
                            dve.wait_ge(g_step[a], step_at(n, k))

                        if k == SQ:
                            if a == 0:
                                dve.wait_ge(ya_ready, m + after(-3))
                                dve.wait_ge(dd0_ready, m + after(-3))
                                dve.tensor_copy(cc[par][:], gcol[:, n, :]).then_inc(cc_ready, 1)
                        elif k == SS:
                            came()
                            dve.wait_ge(rk_ready, m + after(-2))
                            dve.tensor_scalar(qe[a][:], gd[a][:, 0:SH], GD * NORM_EPS, 4 * GD * NORM_EPS ** 2,
                                              ALU.mult, ALU.add)
                            dve.tensor_scalar(kk[a][:], gd[a][:, SH:2 * SH], 4 * NORM_EPS, None, ALU.add).then_inc(kk_ready, 1)
                        elif k == TVK:
                            dve.wait_ge(cc_ready, n + after(0))
                            came()
                            dve.tensor_tensor(vb[:, mine, :], b, wide(cc[par][:, mine], P), ALU.mult)
                            dve.wait_ge(kend_ready, m + after(-2))
                            dve.wait_ge(rk_ready, m + after(0))
                            dve.tensor_tensor(kn[:, mine, :], b2, wide(rk[a][:], P), ALU.mult).then_inc(kn_ready, 1)
                        elif k == GQ:
                            dve.wait_ge(DTb_ready, m + after(0))
                            dve.wait_ge(C_ready[a], n * (LEVELS + 1) + after(-1))
                            came()
                            dve.scalar_tensor_tensor(LT[:, mine, :], b, -1.0, DTb[:, mine, :], ALU.mult, ALU.mult)\
                               .then_inc(LT_ready, 1)
                            dve.wait_ge(C_ready[a], n * (LEVELS + 1) + after(0))
                            dve.scalar_tensor_tensor(XT[:, mine, :], b, -1.0, C[0][:, mine, :], ALU.mult, ALU.mult)\
                               .then_inc(XT0_off_ready, 1)
                            dve.tensor_tensor(intra[:, mine, :], b2, DT[:, mine, :], ALU.mult).then_inc(intra_ready, 1)
                            dve.wait_ge(XT0_off_ready, m + after(0))
                            dve.tensor_tensor(XT[:, mine, :], XT[:, mine, :],
                                              ident[:].unsqueeze(1).broadcast_to([P, SH, P]), ALU.add).then_inc(XT0_ready, 1)
                        elif LEVEL <= k < KS and (k - LEVEL) % 2:
                            lv = (k - LEVEL) // 2
                            width = 2 << lv
                            if lv == 0:
                                dve.wait_ge(X0_ready, m + after(0))
                            else:
                                dve.wait_ge(XT_ready[a], n * LEVELS + after(lv - 1))
                            came()
                            if lv < LEVELS - 1:
                                even = halves(X[:, mine, :], width, 0)
                                dve.tensor_tensor(even, even, blocks(gd8[a][:, 0:SH, :], width), ALU.add)
                            odd = halves(XT[:, mine, :], width, 1)
                            dve.tensor_tensor(odd, odd, blocks(gd8[a][:, SH:2 * SH, :], width), ALU.add).then_inc(XT_ready[a], 1)
                        elif k == KS:
                            came()
                            for i in range(SH):
                                h = a * SH + i
                                last = dve.scalar_tensor_tensor(R2[:, h, :], b[:, i, :], cc[par][:, GH + h:GH + h + 1],
                                                                vb[:, h, :], ALU.mult, ALU.add)
                            last.then_inc(R2_ready, 1)
                        elif k == OD:
                            came()
                            for i in range(SH):
                                h = a * SH + i
                                last = dve.scalar_tensor_tensor(S[:, h, :], S[:, h, :], eg[:, h, P - 1:P], b2[:, i, :],
                                                                ALU.mult, ALU.add)
                            last.then_inc(S_ready, 1)
                        elif k == SUMS:
                            dve.wait_ge(sqo_ready, m + after(0))
                            dve.wait_ge(ro_ready, m + after(-2))
                            dve.reduce_sum(so[a][:], sq[:, mine, :], AX.X).then_inc(so_ready, 1)
                            dve.wait_ge(so_ready, m + after(0))
                            dve.scalar_tensor_tensor(so[a][:], so[a][:], 1.0 / GD, qe[a][:], ALU.mult, ALU.add)\
                               .then_inc(mo_ready, 1)
                        elif k == NORM:
                            dve.wait_ge(ro_ready, m + after(0))
                            dve.tensor_tensor(on[:, mine, :], b, wide(ro[a][:], P), ALU.mult).then_inc(on_ready, 1)
                        elif k == TY:
                            dve.wait_ge(ya_stored[par], it * 32 + (16 * (j // 2) + 16))
                            came()
                            dve.scalar_tensor_tensor(ya[par][:, mine, :], b, half_w[:], za[par][:, mine, :],
                                                     ALU.mult, ALU.mult).then_inc(ya_ready, 1)

                    for s in range(SLOTS):
                        if s < UNITS and s % len(HEAD_UNITS) == 0:
                            hp = s // len(HEAD_UNITS)
                            dve.wait_ge(p_hi_ready, it * UNITS + after(s - 1))
                            dve.tensor_copy(fbias[hp][:], fcol[:, it * 2 + hp, :]).then_inc(fbias_ready, 1)
                        for q in range(PLACES):
                            if q == 1 and s >= LAG and unit(s - LAG)[2] == 4 * unit(s - LAG)[1] + 3:
                                finish(*unit(s - LAG)[0:2])
                            for item in AUX_AT[s][q]:
                                do_aux(item, it)
                            for j, k, a in GDN_AT[s][q]:
                                gdn(j, k, a)


def project_out(nc, io, scr, out):
    TILES = SEQ // P
    with ExitStack() as ctx:
        def sb(name, shape, dt=F32):
            return ctx.enter_context(nc.sbuf_tensor("o_" + name, shape, dt))

        def sem(name):
            return ctx.enter_context(nc.semaphore("o_" + name))

        w_raw = [sb(f"w_raw{i}", [P, D_MODEL]) for i in range(KT)]
        w_hi = sb("w_hi", [P, KT, D_MODEL], F32R)
        w_lo = sb("w_lo", [P, KT, D_MODEL], F32R)
        ln_g, ln_b = sb("ln_g", [P, D_MODEL]), sb("ln_b", [P, D_MODEL])
        y = [sb(f"y{i}", [P, KT, P]) for i in range(2)]
        y_hi = [sb(f"y_hi{i}", [P, KT, P], F32R) for i in range(2)]
        y_lo = [sb(f"y_lo{i}", [P, KT, P], F32R) for i in range(2)]
        x = [sb(f"x{i}", [P, D_MODEL]) for i in range(2)]
        h = [sb(f"h{i}", [P, D_MODEL]) for i in range(2)]
        scaled = [sb(f"scaled{i}", [P, D_MODEL]) for i in range(2)]
        res = [sb(f"res{i}", [P, D_MODEL]) for i in range(2)]
        stats = sb("stats", [P, 2, 6])
        mv = sb("mv", [P, 2])
        rstd0, rstd = sb("rstd0", [P, 1]), sb("rstd", [P, 1])
        half = sb("half", [P, 1])
        banks = [ctx.enter_context(nc.psum_tensor(f"o_bank{i}", [P, D_MODEL], F32)) for i in range(2)]

        w_landed = [sem(f"w_landed{i}") for i in range(KT)]
        w_hi_ready, w_split = sem("w_hi_ready"), sem("w_split")
        ln_landed = sem("ln_landed")
        y_landed = [sem(f"y_landed{i}") for i in range(2)]
        x_landed = [sem(f"x_landed{i}") for i in range(2)]
        half_set = sem("half_set")
        mv_free = sem("mv_free")
        y_hi_ready, y_lo_ready, summed, h_ready = sem("y_hi_ready"), sem("y_lo_ready"), sem("summed"), sem("h_ready")
        stats_ready, mv_ready, var_ready, rstd_ready = (
            sem("stats_ready"), sem("mv_ready"), sem("var_ready"), sem("rstd_ready"))
        normed, scaled_ready, res_ready = sem("normed"), sem("scaled_ready"), sem("res_ready")
        stored = [sem(f"stored{i}") for i in range(2)]
        mixed = scr["mixT"].rearrange("k p (n t) -> n p k t", t=P)
        x_rows = io["x"].rearrange("(n t) d -> n t d", t=P)
        out_rows = out.rearrange("(n t) d -> n t d", t=P)

        with nc.Block() as block:
            @block.sync
            def _(sp):
                for i in range(2):
                    sp.sem_inc(stored[i], 16)

                def load(t, par, first=False):
                    if not first:
                        sp.wait_ge(y_lo_ready, t + after(-2))
                    sp.dma_start(y[par][:], mixed[t]).then_inc(y_landed[par], 16)
                    if not first:
                        sp.wait_ge(h_ready, t + after(-2))
                        sp.dma_start(x[par][:], x_rows[t]).then_inc(x_landed[par], 16)

                load(0, 0, first=True)
                for k in range(KT):
                    sp.dma_start(w_raw[k][:], io["w_out"][k]).then_inc(w_landed[k], 16)
                load(1, 1, first=True)
                for par in range(2):
                    sp.dma_start(x[par][:], x_rows[par]).then_inc(x_landed[par], 16)
                sp.dma_start(ln_g[:], io["ln_g"].broadcast_to([P, D_MODEL])).then_inc(ln_landed, 16)
                sp.dma_start(ln_b[:], io["ln_b"].broadcast_to([P, D_MODEL])).then_inc(ln_landed, 16)

                def store(t, par):
                    sp.wait_ge(res_ready, t + after(0))
                    sp.dma_start(out_rows[t], res[par][:]).then_inc(stored[par], 16)

                with sp.Fori(0, TILES // 2 - 1) as i:
                    for par in range(2):
                        load(i * 2 + (2 + par), par)
                        store(i * 2 + par, par)
                for par in range(2):
                    store(TILES - 2 + par, par)
                for par in range(2):
                    sp.wait_ge(stored[par], 16 + 16 * TILES // 2)

            @block.gpsimd
            def _(pool):
                credit(pool, [rstd_ready, scaled_ready])
                pool.memset(half[:], -0.5).then_inc(half_set, 1)
                pool.wait_ge(half_set, 1)
                pool.wait_ge(ln_landed, 32)
                with pool.Fori(0, TILES // 2) as i:
                    for par in range(2):
                        t = i * 2 + par
                        pool.wait_ge(var_ready, t + after(0))
                        pool.tensor_tensor(rstd[:], rstd0[:], half[:], ALU.pow).then_inc(rstd_ready, 1)
                        pool.wait_ge(normed, t + after(0))
                        pool.wait_ge(res_ready, t + after(-2))
                        pool.tensor_tensor(scaled[par][:], h[par][:], ln_g[:], ALU.mult).then_inc(scaled_ready, 1)

            @block.tensor
            def _(pe):
                credit(pe, [summed])

                def tile(t, par):
                    pe.wait_ge(h_ready, t + after(-2))
                    for k in range(KT):
                        if isinstance(t, int) and t == 0:
                            pe.wait_ge(w_split, k + 1)
                        if k == 0:
                            pe.wait_ge(y_lo_ready, t + after(0))
                        for n, (a, b) in enumerate(((y_hi, w_hi), (y_hi, w_lo), (y_lo, w_hi))):
                            for c in range(D_MODEL // 512):
                                cut = slice(c * 512, (c + 1) * 512)
                                mm = pe.matmul(banks[par][:, cut], a[par][:, k, :], b[:, k, cut],
                                               start=(k == 0 and n == 0), stop=(k == KT - 1 and n == 2))
                    mm.then_inc(summed, 1)

                tile(0, 0)
                tile(1, 1)
                with pe.Fori(1, TILES // 2) as i:
                    for par in range(2):
                        tile(i * 2 + par, par)

            @block.scalar
            def _(act):
                credit(act, [y_hi_ready])
                act.wait_ge(y_landed[0], 16)
                act.activation(y_hi[0][:], y[0][:], ACT.Copy).then_inc(y_hi_ready, 1)
                for k in range(KT):
                    act.wait_ge(w_landed[k], 16)
                    act.activation(w_hi[:, k, :], w_raw[k][:], ACT.Copy).then_inc(w_hi_ready, 1)

                def hi(t, par, landed):
                    act.wait_ge(y_landed[par], landed)
                    act.wait_ge(summed, t + after(-2))
                    act.activation(y_hi[par][:], y[par][:], ACT.Copy).then_inc(y_hi_ready, 1)

                hi(1, 1, 16)
                with act.Fori(1, TILES // 2) as i:
                    for par in range(2):
                        hi(i * 2 + par, par, i * 16 + 16)

            @block.vector
            def _(dve):
                credit(dve, [y_lo_ready, h_ready, stats_ready, mv_ready, var_ready, normed, res_ready])

                def lo(t, par):
                    dve.wait_ge(y_hi_ready, t + after(0))
                    dve.wait_ge(summed, t + after(-2))
                    dve.tensor_tensor(y_lo[par][:], y[par][:], y_hi[par][:].bitcast(F32), ALU.subtract)\
                       .then_inc(y_lo_ready, 1)

                lo(0, 0)
                for k in range(KT):
                    dve.wait_ge(w_hi_ready, k + 1)
                    dve.tensor_tensor(w_lo[:, k, :], w_raw[k][:], w_hi[:, k, :].bitcast(F32), ALU.subtract)\
                       .then_inc(w_split, 1)
                lo(1, 1)

                def norm(t, par, landed):
                    dve.wait_ge(x_landed[par], landed)
                    dve.wait_ge(summed, t + after(0))
                    dve.wait_ge(scaled_ready, t + after(-2))
                    dve.scalar_tensor_tensor(h[par][:], x[par][:], DEEP_ALPHA, banks[par][:], ALU.mult, ALU.add)\
                       .then_inc(h_ready, 1)
                    dve.wait_ge(h_ready, t + after(0))
                    dve.wait_ge(mv_ready, t + after(-1))
                    dve.bn_stats(stats[:, 0, :], h[par][:, 0:512])
                    dve.bn_stats(stats[:, 1, :], h[par][:, 512:]).then_inc(stats_ready, 1)
                    dve.wait_ge(stats_ready, t + after(0))
                    dve.wait_ge(normed, t + after(-1))
                    dve.sem_inc(mv_free, 1)
                    dve.bn_aggr(mv[:], stats[:]).then_inc(mv_ready, 1)
                    dve.wait_ge(mv_ready, t + after(0))
                    dve.wait_ge(rstd_ready, t + after(-1))
                    dve.tensor_scalar(rstd0[:], mv[:, 1:2], LN_EPS, None, ALU.add).then_inc(var_ready, 1)

                def finish(t, par, stored_value):
                    dve.wait_ge(rstd_ready, t + after(0))
                    dve.tensor_scalar(h[par][:], h[par][:], mv[:, 0:1], rstd[:], ALU.subtract, ALU.mult)\
                       .then_inc(normed, 1)
                    dve.wait_ge(scaled_ready, t + after(0))
                    dve.wait_ge(stored[par], stored_value)
                    dve.tensor_tensor(res[par][:], scaled[par][:], ln_b[:], ALU.add).then_inc(res_ready, 1)

                dve.wait_ge(ln_landed, 32)
                with dve.Fori(0, TILES // 2 - 1) as i:
                    for par in range(2):
                        norm(i * 2 + par, par, i * 16 + 16)
                        lo(i * 2 + (par + 2), par)
                        finish(i * 2 + par, par, i * 16 + 16)
                for par in range(2):
                    t = TILES - 2 + par
                    norm(t, par, 16 * TILES // 2)
                    finish(t, par, 16 * TILES // 2)




def build(nc, io, out):
    def scratch(name, shape, dt=F32):
        return nc.dram_tensor("dram_" + name, shape, dt).ap()

    scr = {
        "feat": scratch("feat", (N_FEAT, P, SEQ)),
        "gates": scratch("gates", (GATES, SEQ)),
        "neg_cum": scratch("neg_cum", (FH, SEQ)),
        "mixT": scratch("mixT", (KT, P, SEQ)),
    }
    for n in ("q_hi", "q_lo", "k_hi", "k_lo"):
        scr[n] = scratch(n, (4, P, SEQ))
    project(nc, io, scr)
    mix(nc, io, scr)
    project_out(nc, io, scr, out)


def tiles_of(w, columns):
    return w[:, columns].reshape(KT, P, P).transpose(1, 0, 2).reshape(P, KT * P)


def constants():
    s, c = np.arange(P)[:, None], np.arange(P)[None, :]
    levels = [((s // (2 * b) == c // (2 * b)) & (s // b % 2 == 0) & (c // b % 2 == 1)).astype(np.float32)
              for b in (1, 2, 4, 8, 16, 32, 64)]
    neg = np.float32(NEG)
    return (np.stack(levels + [np.where(c > s, neg, np.float32(0)), np.where(c < s, neg, np.float32(0))], 1),
            np.eye(P, dtype=np.float32))


def kernel(x, w_in, conv_w, a_log, dt_bias, gdn_norm_w, fox_f_bias, w_out, ln_g, ln_b):
    import concourse.bacc as bacc
    from concourse.bass_utils import run_bass_kernel_spmd as run

    GW, FW = GH * GD, FH * FD
    w = np.asarray(w_in)[0]
    beta_at = 4 * GW
    qb_at = beta_at + 2 * GH
    gates = np.zeros((D_MODEL, P), w.dtype)
    gates[:, BETA:BETA + GH] = w[:, beta_at:beta_at + GH]
    gates[:, DECAY:DECAY + GH] = w[:, beta_at + GH:qb_at]
    gates[:, FORGET:FORGET + FH] = w[:, qb_at + 4 * FW:]
    starts = [i * P for i in range(16)] + [qb_at + 3 * FW + i * P for i in range(4)]
    for i in range(4):
        starts += [qb_at + i * P, qb_at + FW + i * P]
    starts += [qb_at + 2 * FW + i * P for i in range(4)]
    masks, ident = constants()
    arrays = {
        "masks": masks,
        "ident": ident,
        "w": np.stack([tiles_of(gates, slice(0, P))] + [tiles_of(w, slice(s, s + P)) for s in starts]),
        "xT": np.ascontiguousarray(np.asarray(x)[0].T.reshape(KT, P, SEQ)),
        "x": np.ascontiguousarray(np.asarray(x)[0]),
        "taps": np.ascontiguousarray(np.asarray(conv_w)[0].reshape(CONV_K, 12, P).transpose(2, 1, 0)),
        "dt_bias": np.asarray(dt_bias).reshape(GH, 1),
        "a_log": np.asarray(a_log).reshape(GH, 1),
        "f_bias": np.asarray(fox_f_bias).reshape(FH, 1),
        "norm_w": np.asarray(gdn_norm_w).reshape(GD, 1),
        "w_out": np.ascontiguousarray(np.asarray(w_out)[0].reshape(KT, P, D_MODEL)),
        "ln_g": np.asarray(ln_g).reshape(1, D_MODEL),
        "ln_b": np.asarray(ln_b).reshape(1, D_MODEL),
    }
    nc = bacc.Bacc("TRN2", target_bir_lowering=False, num_devices=1)
    io = {n: nc.dram_tensor("in_" + n, a.shape, F32, kind="ExternalInput").ap() for n, a in arrays.items()}
    out = nc.dram_tensor("out", (SEQ, D_MODEL), F32, kind="ExternalOutput").ap()
    build(nc, io, out)
    r = run(nc, [{"in_" + n: a for n, a in arrays.items()}], core_ids=[0])
    return r.results[0]["out"].reshape(1, SEQ, D_MODEL)
```
